# Optimizing a Trainium2 kernel written in Bass

```python
import jax, jax.numpy as jnp
from jax import lax
import numpy as np
import jax
import jax.numpy as jnp

D_MODEL = 1024
BATCH = 1
SEQ = 256
DEPTH = 1

GRID_W = 64
CTX_LEN = 256
CHUNK = 128
RET_HEADS = 4
RET_DK = 128
RET_DV = 128
ML_HEADS = 4
ML_DH = 128
RET_W = RET_HEADS * RET_DK
RET_VW = RET_HEADS * RET_DV
ML_W = ML_HEADS * ML_DH
N_ML_GATES = 4 * ML_HEADS
FFN_HIDDEN = -((-8 * D_MODEL) // (3 * 256)) * 256
ROPE_BASE = 10000.0
EPS = 1e-6
IN_WIDTHS = (RET_W, RET_W, RET_VW, RET_VW, ML_W, ML_W, ML_W, ML_W, N_ML_GATES, D_MODEL, D_MODEL)
IN_COLS = sum(IN_WIDTHS)


def rms_norm(x, gain):
    xf = x.astype(jnp.float32)
    y = xf * lax.rsqrt(jnp.mean(xf * xf, axis=-1, keepdims=True) + EPS)
    return (y * gain.astype(jnp.float32)).astype(x.dtype)

def head_norm(t):
    tf = t.astype(jnp.float32)
    return tf * lax.rsqrt(jnp.mean(tf * tf, axis=-1, keepdims=True) + EPS)

def modulate(h, shift, scale):
    return h * (1 + scale) + shift

def to_heads(t, n_heads):
    b, n, _ = t.shape
    return t.reshape(b, n, n_heads, -1).transpose(0, 2, 1, 3)

def from_heads(t):
    b, h, n, d = t.shape
    return t.transpose(0, 2, 1, 3).reshape(b, n, h * d)

def rope_2d(n):
    n_rows = n // GRID_W
    rows = jnp.broadcast_to(jnp.arange(n_rows, dtype=jnp.float32)[:, None], (n_rows, GRID_W)).reshape(n)
    cols = jnp.broadcast_to(jnp.arange(GRID_W, dtype=jnp.float32)[None, :], (n_rows, GRID_W)).reshape(n)
    n_freq = RET_DK // 4
    inv = ROPE_BASE ** (-jnp.arange(n_freq, dtype=jnp.float32) / n_freq)
    ang = jnp.concatenate([rows[:, None] * inv, cols[:, None] * inv], axis=-1)
    return jnp.cos(ang), jnp.sin(ang)

def apply_rope(t, cos, sin):
    half = t.shape[-1] // 2
    t1, t2 = t[..., :half], t[..., half:]
    cos = cos.astype(t.dtype)
    sin = sin.astype(t.dtype)
    return jnp.concatenate([t1 * cos - t2 * sin, t2 * cos + t1 * sin], axis=-1)

def to_chunks(t):
    b, h, n = t.shape[:3]
    t = t.reshape(b, h, n // CHUNK, CHUNK, *t.shape[3:])
    return jnp.moveaxis(t, 2, 0)

def from_chunks(t):
    t = jnp.moveaxis(t, 0, 2)
    b, h, nc, l = t.shape[:4]
    return t.reshape(b, h, nc * l, *t.shape[4:])

def retention_scan(q, k, v, log_gamma, state):
    q, k, v = (t.astype(jnp.float32) for t in (q, k, v))
    lg = log_gamma.astype(jnp.float32)
    pos = jnp.arange(CHUNK, dtype=jnp.float32)
    rel = pos[:, None] - pos[None, :]
    intra = jnp.where(rel >= 0, jnp.exp(lg[:, None, None] * jnp.maximum(rel, 0.0)), 0.0)
    inter = jnp.exp(lg[:, None] * (pos + 1.0))
    to_end = jnp.exp(lg[:, None] * (CHUNK - 1.0 - pos))
    chunk_decay = jnp.exp(lg * CHUNK)

    def step(s, inp):
        qc, kc, vc = inp
        scores = jnp.einsum("bhld,bhsd->bhls", qc, kc) * intra
        out = jnp.einsum("bhls,bhsv->bhlv", scores, vc) + inter[..., None] * jnp.einsum("bhld,bhdv->bhlv", qc, s)
        s_new = chunk_decay[:, None, None] * s + jnp.einsum("bhsd,bhsv->bhdv", kc * to_end[..., None], vc)
        return s_new, out

    final, outs = lax.scan(step, state, (to_chunks(q), to_chunks(k), to_chunks(v)))
    return from_chunks(outs), final

def mlstm_scan(q, k, v, i_pre, log_f, state):
    q, k, v, i_pre, log_f = (t.astype(jnp.float32) for t in (q, k, v, i_pre, log_f))
    causal = jnp.tril(jnp.ones((CHUNK, CHUNK), dtype=bool))

    def step(carry, inp):
        c_mat, n_vec, m = carry
        qc, kc, vc, ic, fc = inp
        b_cum = jnp.cumsum(fc, axis=-1)
        log_inter = b_cum + m[..., None]
        log_intra = jnp.where(causal, b_cum[..., :, None] - b_cum[..., None, :] + ic[..., None, :], -jnp.inf)
        m_t = jnp.maximum(log_inter, jnp.max(log_intra, axis=-1))
        w_inter = jnp.exp(log_inter - m_t)
        w_intra = jnp.exp(log_intra - m_t[..., None])
        s = jnp.einsum("bhld,bhsd->bhls", qc, kc) * w_intra
        num = jnp.einsum("bhls,bhsv->bhlv", s, vc) + w_inter[..., None] * jnp.einsum("bhvd,bhld->bhlv", c_mat, qc)
        den = jnp.sum(s, axis=-1) + w_inter * jnp.einsum("bhd,bhld->bhl", n_vec, qc)
        h = num / jnp.maximum(jnp.abs(den), jnp.exp(-m_t))[..., None]
        b_last = b_cum[..., -1]
        log_src = b_last[..., None] - b_cum + ic
        m_new = jnp.maximum(b_last + m, jnp.max(log_src, axis=-1))
        w_old = jnp.exp(b_last + m - m_new)
        w_src = jnp.exp(log_src - m_new[..., None])
        c_new = w_old[..., None, None] * c_mat + jnp.einsum("bhs,bhsv,bhsd->bhvd", w_src, vc, kc)
        n_new = w_old[..., None] * n_vec + jnp.einsum("bhs,bhsd->bhd", w_src, kc)
        return (c_new, n_new, m_new), h

    final, outs = lax.scan(step, state, tuple(to_chunks(t) for t in (q, k, v, i_pre, log_f)))
    return from_chunks(outs), final

def zero_states(b):
    ret = jnp.zeros((b, RET_HEADS, RET_DK, RET_DV), jnp.float32)
    ml = (jnp.zeros((b, ML_HEADS, ML_DH, ML_DH), jnp.float32),
          jnp.zeros((b, ML_HEADS, ML_DH), jnp.float32),
          jnp.zeros((b, ML_HEADS), jnp.float32))
    return (ret, ml)

def mixer_inputs(h, w_in, gate_bias, rope):
    offsets = np.cumsum(IN_WIDTHS)[:-1].tolist()
    rq, rk, rv, rg, mq, mk, mv, mo, mg, bg_ret, bg_ml = (h @ w for w in jnp.split(w_in, offsets, axis=-1))
    rq = to_heads(rq, RET_HEADS)
    rk = to_heads(rk, RET_HEADS) * (RET_DK ** -0.5)
    if rope is not None:
        rq = apply_rope(rq, *rope)
        rk = apply_rope(rk, *rope)
    rv = to_heads(rv, RET_HEADS)
    mq = to_heads(mq, ML_HEADS)
    mk = to_heads(mk, ML_HEADS) * (ML_DH ** -0.5)
    mv = to_heads(mv, ML_HEADS)
    b, n, _ = mg.shape
    mg = (mg + gate_bias.reshape(-1)).reshape(b, n, 4, ML_HEADS).transpose(2, 0, 3, 1)
    i_f, lf_f, i_b, lf_b = mg[0], jax.nn.log_sigmoid(mg[1]), mg[2], jax.nn.log_sigmoid(mg[3])
    feats = (rq, rk, rv, mq, mk, mv, i_f, lf_f, i_b, lf_b)
    post = (rg, mo, bg_ret, bg_ml)
    return feats, post

def bidirectional_scans(feats, log_gamma, st_f, st_b):
    rq, rk, rv, mq, mk, mv, i_f, lf_f, i_b, lf_b = feats
    flip = lambda t: jnp.flip(t, axis=2)
    ret_f, r_state_f = retention_scan(rq, rk, rv, log_gamma[0], st_f[0])
    ml_f, m_state_f = mlstm_scan(mq, mk, mv, i_f, lf_f, st_f[1])
    ret_b, r_state_b = retention_scan(flip(rq), flip(rk), flip(rv), log_gamma[1], st_b[0])
    ml_b, m_state_b = mlstm_scan(flip(mq), flip(mk), flip(mv), flip(i_b), flip(lf_b), st_b[1])
    return ret_f + flip(ret_b), ml_f + flip(ml_b), (r_state_f, m_state_f), (r_state_b, m_state_b)

def mixer_output(ret, ml, rg, mo, bg_ret, bg_ml, w_ret_up, w_ml_up, w_out):
    dtype = rg.dtype
    y_ret = from_heads(head_norm(ret)).astype(dtype) * jax.nn.silu(rg)
    y_ml = from_heads(head_norm(jax.nn.sigmoid(to_heads(mo, ML_HEADS)) * ml)).astype(dtype)
    merged = jax.nn.sigmoid(bg_ret) * (y_ret @ w_ret_up) + jax.nn.sigmoid(bg_ml) * (y_ml @ w_ml_up)
    return merged @ w_out

def swiglu(h, w_ffn_in, w_ffn_out):
    gate, up = jnp.split(h @ w_ffn_in, 2, axis=-1)
    return (jax.nn.silu(gate) * up) @ w_ffn_out

def first_inputs(seed: int = 0) -> dict:
    key = jax.random.key(seed)
    ks = jax.random.split(key, 20)
    f32 = jnp.float32

    def nrm(k, shape, scale):
        return jax.random.normal(k, shape, f32) * scale

    x = nrm(ks[0], (BATCH, SEQ, D_MODEL), 1.0)
    c = nrm(ks[1], (BATCH, D_MODEL), 1.0)
    ctx = nrm(ks[2], (BATCH, CTX_LEN, D_MODEL), 1.0)
    c_ctx = nrm(ks[3], (D_MODEL,), 1.0)
    w_ada = nrm(ks[4], (DEPTH, D_MODEL, 6 * D_MODEL), 0.5 * D_MODEL ** -0.5)
    b_ada = nrm(ks[5], (DEPTH, 6 * D_MODEL), 0.02)
    norm1_gain = 1.0 + nrm(ks[6], (DEPTH, D_MODEL), 0.02)
    norm2_gain = 1.0 + nrm(ks[7], (DEPTH, D_MODEL), 0.02)
    w_in = nrm(ks[8], (DEPTH, D_MODEL, IN_COLS), D_MODEL ** -0.5)
    i_bias = nrm(ks[9], (DEPTH, 2, ML_HEADS), 0.1)
    f_bias = jnp.linspace(3.0, 6.0, ML_HEADS, dtype=f32) + nrm(ks[10], (DEPTH, 2, ML_HEADS), 0.1)
    mlstm_gate_bias = jnp.stack([i_bias[:, 0], f_bias[:, 0], i_bias[:, 1], f_bias[:, 1]], axis=1)
    gamma = 1.0 - 2.0 ** (-5.0 - jnp.arange(RET_HEADS, dtype=f32))
    ret_decay_logit = jnp.log(gamma / (1.0 - gamma)) + nrm(ks[11], (DEPTH, 2, RET_HEADS), 0.1)
    w_ret_up = nrm(ks[12], (DEPTH, RET_VW, D_MODEL), RET_VW ** -0.5)
    w_ml_up = nrm(ks[13], (DEPTH, ML_W, D_MODEL), ML_W ** -0.5)
    w_out = nrm(ks[14], (DEPTH, D_MODEL, D_MODEL), D_MODEL ** -0.5)
    w_ffn_in = nrm(ks[15], (DEPTH, D_MODEL, 2 * FFN_HIDDEN), D_MODEL ** -0.5)
    w_ffn_out = nrm(ks[16], (DEPTH, FFN_HIDDEN, D_MODEL), FFN_HIDDEN ** -0.5)
    final_gain = 1.0 + nrm(ks[17], (D_MODEL,), 0.02)
    return {"x": x, "c": c, "ctx": ctx, "c_ctx": c_ctx, "w_ada": w_ada, "b_ada": b_ada,
            "norm1_gain": norm1_gain, "norm2_gain": norm2_gain, "w_in": w_in,
            "mlstm_gate_bias": mlstm_gate_bias, "ret_decay_logit": ret_decay_logit,
            "w_ret_up": w_ret_up, "w_ml_up": w_ml_up, "w_out": w_out,
            "w_ffn_in": w_ffn_in, "w_ffn_out": w_ffn_out, "final_gain": final_gain}

def first_block(x, c, ctx, c_ctx, w_ada, b_ada, norm1_gain, norm2_gain, w_in, mlstm_gate_bias,
              ret_decay_logit, w_ret_up, w_ml_up, w_out, w_ffn_in, w_ffn_out, final_gain):
    b, n, _ = x.shape
    rope = rope_2d(n)
    log_gamma = jax.nn.log_sigmoid(ret_decay_logit.astype(jnp.float32))
    for layer in range(DEPTH):
        mod = jax.nn.silu(c) @ w_ada[layer] + b_ada[layer]
        sh1, sc1, g1, sh2, sc2, g2 = jnp.split(mod[:, None, :], 6, axis=-1)
        mod_c = jax.nn.silu(c_ctx) @ w_ada[layer] + b_ada[layer]
        csh1, csc1, cg1, csh2, csc2, cg2 = jnp.split(mod_c, 6)

        hc = modulate(rms_norm(ctx, norm1_gain[layer]), csh1, csc1)
        feats_c, post_c = mixer_inputs(hc, w_in[layer], mlstm_gate_bias[layer], None)
        zero = zero_states(b)
        ret_c, ml_c, st_f, st_b = bidirectional_scans(feats_c, log_gamma[layer], zero, zero)

        hx = modulate(rms_norm(x, norm1_gain[layer]), sh1, sc1)
        feats_x, post_x = mixer_inputs(hx, w_in[layer], mlstm_gate_bias[layer], rope)
        ret_x, ml_x, _, _ = bidirectional_scans(feats_x, log_gamma[layer], st_f, st_b)
        x = x + g1 * mixer_output(ret_x, ml_x, *post_x, w_ret_up[layer], w_ml_up[layer], w_out[layer])
        x = x + g2 * swiglu(modulate(rms_norm(x, norm2_gain[layer]), sh2, sc2), w_ffn_in[layer], w_ffn_out[layer])

        if layer + 1 < DEPTH:
            ctx = ctx + cg1 * mixer_output(ret_c, ml_c, *post_c, w_ret_up[layer], w_ml_up[layer], w_out[layer])
            ctx = ctx + cg2 * swiglu(modulate(rms_norm(ctx, norm2_gain[layer]), csh2, csc2),
                                     w_ffn_in[layer], w_ffn_out[layer])
    return rms_norm(x, final_gain)


DEPTH_2 = 2

NORM_EPS = 1e-6
NEG_INF = -1e30

A_HEADS = 8
A_KV_HEADS = 2
A_HEAD_DIM = 64
WINDOW = 128
A_BLOCK = 128
B_WIDTH = 512
B_GROUPS = 4
B_CHUNK = 128
C_HEADS = 8
C_Q_LORA = 384
C_KV_LORA = 256
C_NOPE = 64
C_ROPE = 32
C_V = 64
C_BLOCK = 128
D_WIDTH = 512
D_CONV = 3
N_EXPERTS = 16
EXPERT_FF = 1024
EC_FACTOR = 2

A_Q_W = A_HEADS * A_HEAD_DIM
A_KV_W = A_KV_HEADS * A_HEAD_DIM
EVEN_CTX_COLS = 2 * A_KV_W
EVEN_IN = EVEN_CTX_COLS + A_Q_W + 2 * B_WIDTH
EVEN_OUT = A_Q_W + B_WIDTH
ODD_CTX_COLS = C_KV_LORA + C_ROPE
ODD_IN = ODD_CTX_COLS + C_Q_LORA + 3 * D_WIDTH
ODD_OUT = C_HEADS * C_V + D_WIDTH
N_EVEN = (DEPTH_2 + 1) // 2
N_ODD = DEPTH_2 // 2


def rms_norm_2(x, g):
    xf = x.astype(jnp.float32)
    y = xf * lax.rsqrt(jnp.mean(xf * xf, axis=-1, keepdims=True) + NORM_EPS)
    return (y * g.astype(jnp.float32)).astype(x.dtype)

def layer_norm(x, g):
    xf = x.astype(jnp.float32)
    mu = jnp.mean(xf, axis=-1, keepdims=True)
    var = jnp.mean(jnp.square(xf - mu), axis=-1, keepdims=True)
    return ((xf - mu) * lax.rsqrt(var + NORM_EPS) * g.astype(jnp.float32)).astype(x.dtype)

def axial_rope_tables(rows, rot_dim):
    row = jnp.repeat(jnp.arange(rows, dtype=jnp.float32), GRID_W)
    col = jnp.tile(jnp.arange(GRID_W, dtype=jnp.float32), rows)
    n_freq = rot_dim // 4
    inv_freq = ROPE_BASE ** (-jnp.arange(n_freq, dtype=jnp.float32) / n_freq)
    ang = jnp.concatenate([row[:, None] * inv_freq[None, :], col[:, None] * inv_freq[None, :]], axis=-1)
    return jnp.cos(ang), jnp.sin(ang)

def apply_rope_2(x, cos, sin):
    x1, x2 = jnp.split(x, 2, axis=-1)
    cs = cos[None, :, None, :].astype(x.dtype)
    sn = sin[None, :, None, :].astype(x.dtype)
    return jnp.concatenate([x1 * cs - x2 * sn, x2 * cs + x1 * sn], axis=-1)

def gqa_attend(q, k, v, mask, sink, scale):
    s = jnp.einsum('bqhgd,bkhd->bhgqk', q, k).astype(jnp.float32) * scale
    if mask is not None:
        s = jnp.where(mask, s, NEG_INF)
    if sink is not None:
        sk = jnp.broadcast_to(sink.astype(jnp.float32)[None, :, :, None, None], s.shape[:-1] + (1,))
        s = jnp.concatenate([s, sk], axis=-1)
    p = jax.nn.softmax(s, axis=-1)
    if sink is not None:
        p = p[..., :-1]
    return jnp.einsum('bhgqk,bkhd->bqhgd', p.astype(v.dtype), v)

def window_attention(q, k, v, k_ctx, v_ctx, sink_g, scale):
    bsz, n = q.shape[0], q.shape[1]
    g = A_HEADS // A_KV_HEADS
    nb = n // A_BLOCK
    span = A_BLOCK + 2 * WINDOW
    pad = ((0, 0), (WINDOW, WINDOW), (0, 0), (0, 0))
    kp = jnp.pad(k, pad)
    vp = jnp.pad(v, pad)
    qi = jnp.arange(A_BLOCK)
    kj = jnp.arange(span)
    band = jnp.abs(kj[None, :] - WINDOW - qi[:, None]) <= WINDOW
    ctx_ok = jnp.ones((A_BLOCK, k_ctx.shape[1]), dtype=jnp.bool_)

    def block(nidx):
        start = nidx * A_BLOCK
        qb = lax.dynamic_slice_in_dim(q, start, A_BLOCK, axis=1).reshape(bsz, A_BLOCK, A_KV_HEADS, g, A_HEAD_DIM)
        kb = lax.dynamic_slice_in_dim(kp, start, span, axis=1)
        vb = lax.dynamic_slice_in_dim(vp, start, span, axis=1)
        kpos = start - WINDOW + kj
        mask = band & ((kpos >= 0) & (kpos < n))[None, :]
        mask = jnp.concatenate([mask, ctx_ok], axis=1)
        o = gqa_attend(qb, jnp.concatenate([kb, k_ctx], axis=1), jnp.concatenate([vb, v_ctx], axis=1), mask, sink_g, scale)
        return o.reshape(bsz, A_BLOCK, A_Q_W)

    out = lax.map(block, jnp.arange(nb))
    return jnp.moveaxis(out, 0, 1).reshape(bsz, n, A_Q_W)

def dense_block_attention(q, k_all, v_all, scale):
    bsz, n, h, _ = q.shape
    dv = v_all.shape[-1]
    nb = n // C_BLOCK

    def block(nidx):
        qb = lax.dynamic_slice_in_dim(q, nidx * C_BLOCK, C_BLOCK, axis=1)
        return gqa_attend(qb[:, :, :, None], k_all, v_all, None, None, scale)[:, :, :, 0]

    out = lax.map(block, jnp.arange(nb))
    return jnp.moveaxis(out, 0, 1).reshape(bsz, n, h * dv)

def spatial_gating(z, norm_g, w_s, b_s):
    bsz, n, _ = z.shape
    u, v = jnp.split(jax.nn.gelu(z), 2, axis=-1)
    v = layer_norm(v, norm_g)
    vc = v.reshape(bsz, n // B_CHUNK, B_CHUNK, B_GROUPS, B_WIDTH // B_GROUPS)
    mixed = jnp.einsum('gpq,bcqgd->bcpgd', w_s, vc) + b_s.T[None, None, :, :, None]
    return u * mixed.reshape(bsz, n, B_WIDTH)

def gated_short_conv(z, conv_w):
    gb, gc, hh = jnp.split(z, 3, axis=-1)
    u = gc * hh
    n = u.shape[1]
    half = D_CONV // 2
    up = jnp.pad(u, ((0, 0), (half, half), (0, 0)))
    conv = sum(up[:, j:j + n] * conv_w[j] for j in range(D_CONV))
    return gb * conv

def mla_q(cq, q_norm_g, w_uq, cos, sin):
    bsz, n, _ = cq.shape
    q = (rms_norm_2(cq, q_norm_g) @ w_uq).reshape(bsz, n, C_HEADS, C_NOPE + C_ROPE)
    q_nope, q_rope = q[..., :C_NOPE], q[..., C_NOPE:]
    if cos is not None:
        q_rope = apply_rope_2(q_rope, cos, sin)
    return jnp.concatenate([q_nope, q_rope], axis=-1)

def mla_kv(ckv, kr, kv_norm_g, w_ukv, cos, sin):
    bsz, n, _ = ckv.shape
    kv = (rms_norm_2(ckv, kv_norm_g) @ w_ukv).reshape(bsz, n, C_HEADS, C_NOPE + C_V)
    k_nope, v = kv[..., :C_NOPE], kv[..., C_NOPE:]
    kr = kr[:, :, None, :]
    if cos is not None:
        kr = apply_rope_2(kr, cos, sin)
    k = jnp.concatenate([k_nope, jnp.broadcast_to(kr, (bsz, n, C_HEADS, C_ROPE))], axis=-1)
    return k, v

def even_mixer(h_lat, h_ctx, w_in, sink, sgu_norm_g, sgu_w, sgu_b, w_out, cos, sin, need_ctx):
    bsz, n_lat, _ = h_lat.shape
    n_ctx = h_ctx.shape[1]
    g = A_HEADS // A_KV_HEADS
    scale = A_HEAD_DIM ** -0.5
    sink_g = sink.reshape(A_KV_HEADS, g)
    z_lat = h_lat @ w_in
    z_ctx = h_ctx @ (w_in if need_ctx else w_in[:, :EVEN_CTX_COLS])
    k_ctx = z_ctx[..., :A_KV_W].reshape(bsz, n_ctx, A_KV_HEADS, A_HEAD_DIM)
    v_ctx = z_ctx[..., A_KV_W:EVEN_CTX_COLS].reshape(bsz, n_ctx, A_KV_HEADS, A_HEAD_DIM)
    k_lat = apply_rope_2(z_lat[..., :A_KV_W].reshape(bsz, n_lat, A_KV_HEADS, A_HEAD_DIM), cos, sin)
    v_lat = z_lat[..., A_KV_W:EVEN_CTX_COLS].reshape(bsz, n_lat, A_KV_HEADS, A_HEAD_DIM)
    q_lat = apply_rope_2(z_lat[..., EVEN_CTX_COLS:EVEN_CTX_COLS + A_Q_W].reshape(bsz, n_lat, A_HEADS, A_HEAD_DIM), cos, sin)
    o_lat = window_attention(q_lat, k_lat, v_lat, k_ctx, v_ctx, sink_g, scale)
    s_lat = spatial_gating(z_lat[..., EVEN_CTX_COLS + A_Q_W:], sgu_norm_g, sgu_w, sgu_b)
    y_lat = jnp.concatenate([o_lat, s_lat], axis=-1) @ w_out
    if not need_ctx:
        return y_lat, None
    q_ctx = z_ctx[..., EVEN_CTX_COLS:EVEN_CTX_COLS + A_Q_W].reshape(bsz, n_ctx, A_KV_HEADS, g, A_HEAD_DIM)
    o_ctx = gqa_attend(q_ctx, k_ctx, v_ctx, None, sink_g, scale).reshape(bsz, n_ctx, A_Q_W)
    s_ctx = spatial_gating(z_ctx[..., EVEN_CTX_COLS + A_Q_W:], sgu_norm_g, sgu_w, sgu_b)
    y_ctx = jnp.concatenate([o_ctx, s_ctx], axis=-1) @ w_out
    return y_lat, y_ctx

def odd_mixer(h_lat, h_ctx, w_in, q_norm_g, w_uq, kv_norm_g, w_ukv, conv_w, w_out, cos, sin, need_ctx):
    bsz, n_ctx = h_ctx.shape[0], h_ctx.shape[1]
    scale = (C_NOPE + C_ROPE) ** -0.5
    z_lat = h_lat @ w_in
    z_ctx = h_ctx @ (w_in if need_ctx else w_in[:, :ODD_CTX_COLS])
    k_ctx, v_ctx = mla_kv(z_ctx[..., :C_KV_LORA], z_ctx[..., C_KV_LORA:ODD_CTX_COLS], kv_norm_g, w_ukv, None, None)
    k_lat, v_lat = mla_kv(z_lat[..., :C_KV_LORA], z_lat[..., C_KV_LORA:ODD_CTX_COLS], kv_norm_g, w_ukv, cos, sin)
    q_lat = mla_q(z_lat[..., ODD_CTX_COLS:ODD_CTX_COLS + C_Q_LORA], q_norm_g, w_uq, cos, sin)
    k_all = jnp.concatenate([k_lat, k_ctx], axis=1)
    v_all = jnp.concatenate([v_lat, v_ctx], axis=1)
    o_lat = dense_block_attention(q_lat, k_all, v_all, scale)
    c_lat = gated_short_conv(z_lat[..., ODD_CTX_COLS + C_Q_LORA:], conv_w)
    y_lat = jnp.concatenate([o_lat, c_lat], axis=-1) @ w_out
    if not need_ctx:
        return y_lat, None
    q_ctx = mla_q(z_ctx[..., ODD_CTX_COLS:ODD_CTX_COLS + C_Q_LORA], q_norm_g, w_uq, None, None)
    o_ctx = gqa_attend(q_ctx[:, :, :, None], k_ctx, v_ctx, None, None, scale)[:, :, :, 0].reshape(bsz, n_ctx, C_HEADS * C_V)
    c_ctx_out = gated_short_conv(z_ctx[..., ODD_CTX_COLS + C_Q_LORA:], conv_w)
    y_ctx = jnp.concatenate([o_ctx, c_ctx_out], axis=-1) @ w_out
    return y_lat, y_ctx

def expert_choice_ffn(h, w_router, w1, w3, w2):
    n_tok, d = h.shape[1], h.shape[2]
    cap = EC_FACTOR * n_tok // N_EXPERTS
    aff = jax.nn.softmax(jnp.einsum('bnd,de->bne', h, w_router).astype(jnp.float32), axis=-1)
    gate, idx = lax.top_k(jnp.swapaxes(aff, 1, 2), cap)
    xs = jax.vmap(lambda hb, ib: hb[ib])(h, idx)
    a = jnp.einsum('becd,edf->becf', xs, w1)
    b = jnp.einsum('becd,edf->becf', xs, w3)
    y = jnp.einsum('becf,efd->becd', jax.nn.silu(a) * b, w2) * gate[..., None].astype(h.dtype)

    def combine(yb, ib):
        return jnp.zeros((n_tok, d), h.dtype).at[ib.reshape(-1)].add(yb.reshape(-1, d))

    return jax.vmap(combine)(y, idx)

def second_inputs(seed: int = 0) -> dict:
    key = jax.random.key(seed)
    ks = iter(jax.random.split(key, 32))
    D = D_MODEL

    def nrm(shape, scale):
        return jax.random.normal(next(ks), shape, jnp.float32) * scale

    return {
        'x': nrm((BATCH, SEQ, D), 1.0),
        'c': nrm((BATCH, D), 1.0),
        'ctx': nrm((BATCH, CTX_LEN, D), 1.0),
        'c_ctx': nrm((D,), 1.0),
        'mod_w': nrm((DEPTH_2, D, 6 * D), 0.5 * D ** -0.5),
        'mod_b': nrm((DEPTH_2, 6 * D), 0.01),
        'norm1_g': 1.0 + nrm((DEPTH_2, D), 0.05),
        'norm2_g': 1.0 + nrm((DEPTH_2, D), 0.05),
        'ev_w_in': nrm((N_EVEN, D, EVEN_IN), D ** -0.5),
        'ev_sink': nrm((N_EVEN, A_HEADS), 0.5),
        'ev_sgu_norm_g': 1.0 + nrm((N_EVEN, B_WIDTH), 0.05),
        'ev_sgu_w': nrm((N_EVEN, B_GROUPS, B_CHUNK, B_CHUNK), B_CHUNK ** -0.5),
        'ev_sgu_b': nrm((N_EVEN, B_GROUPS, B_CHUNK), 0.1),
        'ev_w_out': nrm((N_EVEN, EVEN_OUT, D), EVEN_OUT ** -0.5),
        'od_w_in': nrm((N_ODD, D, ODD_IN), D ** -0.5),
        'od_q_norm_g': 1.0 + nrm((N_ODD, C_Q_LORA), 0.05),
        'od_w_uq': nrm((N_ODD, C_Q_LORA, C_HEADS * (C_NOPE + C_ROPE)), C_Q_LORA ** -0.5),
        'od_kv_norm_g': 1.0 + nrm((N_ODD, C_KV_LORA), 0.05),
        'od_w_ukv': nrm((N_ODD, C_KV_LORA, C_HEADS * (C_NOPE + C_V)), C_KV_LORA ** -0.5),
        'od_conv_w': nrm((N_ODD, D_CONV, D_WIDTH), D_CONV ** -0.5),
        'od_w_out': nrm((N_ODD, ODD_OUT, D), ODD_OUT ** -0.5),
        'router_w': nrm((DEPTH_2, D, N_EXPERTS), D ** -0.5),
        'exp_w1': nrm((DEPTH_2, N_EXPERTS, D, EXPERT_FF), D ** -0.5),
        'exp_w3': nrm((DEPTH_2, N_EXPERTS, D, EXPERT_FF), D ** -0.5),
        'exp_w2': nrm((DEPTH_2, N_EXPERTS, EXPERT_FF, D), EXPERT_FF ** -0.5),
        'final_g': 1.0 + nrm((D,), 0.05),
    }

def second_block(x, c, ctx, c_ctx, mod_w, mod_b, norm1_g, norm2_g, ev_w_in, ev_sink, ev_sgu_norm_g, ev_sgu_w, ev_sgu_b, ev_w_out, od_w_in, od_q_norm_g, od_w_uq, od_kv_norm_g, od_w_ukv, od_conv_w, od_w_out, router_w, exp_w1, exp_w3, exp_w2, final_g):
    rows = x.shape[1] // GRID_W
    cos_a, sin_a = axial_rope_tables(rows, A_HEAD_DIM)
    cos_c, sin_c = axial_rope_tables(rows, C_ROPE)
    silu_c = jax.nn.silu(c)
    silu_cc = jax.nn.silu(c_ctx)[None, :]
    x_lat, x_ctx = x, ctx
    for layer in range(DEPTH_2):
        need_ctx = layer < DEPTH_2 - 1
        m_lat = jnp.split((silu_c @ mod_w[layer] + mod_b[layer])[:, None, :], 6, axis=-1)
        m_ctx = jnp.split((silu_cc @ mod_w[layer] + mod_b[layer])[:, None, :], 6, axis=-1)
        h_lat = rms_norm_2(x_lat, norm1_g[layer]) * (1 + m_lat[1]) + m_lat[0]
        h_ctx = rms_norm_2(x_ctx, norm1_g[layer]) * (1 + m_ctx[1]) + m_ctx[0]
        i = layer // 2
        if layer % 2 == 0:
            y_lat, y_ctx = even_mixer(h_lat, h_ctx, ev_w_in[i], ev_sink[i], ev_sgu_norm_g[i], ev_sgu_w[i], ev_sgu_b[i], ev_w_out[i], cos_a, sin_a, need_ctx)
        else:
            y_lat, y_ctx = odd_mixer(h_lat, h_ctx, od_w_in[i], od_q_norm_g[i], od_w_uq[i], od_kv_norm_g[i], od_w_ukv[i], od_conv_w[i], od_w_out[i], cos_c, sin_c, need_ctx)
        x_lat = x_lat + m_lat[2] * y_lat
        h_lat = rms_norm_2(x_lat, norm2_g[layer]) * (1 + m_lat[4]) + m_lat[3]
        x_lat = x_lat + m_lat[5] * expert_choice_ffn(h_lat, router_w[layer], exp_w1[layer], exp_w3[layer], exp_w2[layer])
        if need_ctx:
            x_ctx = x_ctx + m_ctx[2] * y_ctx
            h_ctx = rms_norm_2(x_ctx, norm2_g[layer]) * (1 + m_ctx[4]) + m_ctx[3]
            x_ctx = x_ctx + m_ctx[5] * expert_choice_ffn(h_ctx, router_w[layer], exp_w1[layer], exp_w3[layer], exp_w2[layer])
    return rms_norm_2(x_lat, final_g)


def setup_inputs(seed=0):
    out = dict(first_inputs(seed))
    for name, value in second_inputs(seed + 1).items():
        if name != "x":
            out[name + "_2"] = value
    return out


def reference(
    x, c, ctx, c_ctx, w_ada, b_ada, norm1_gain, norm2_gain, w_in, mlstm_gate_bias,
    ret_decay_logit, w_ret_up, w_ml_up, w_out, w_ffn_in, w_ffn_out, final_gain, c_2, ctx_2,
    c_ctx_2, mod_w_2, mod_b_2, norm1_g_2, norm2_g_2, ev_w_in_2, ev_sink_2, ev_sgu_norm_g_2,
    ev_sgu_w_2, ev_sgu_b_2, ev_w_out_2, od_w_in_2, od_q_norm_g_2, od_w_uq_2, od_kv_norm_g_2,
    od_w_ukv_2, od_conv_w_2, od_w_out_2, router_w_2, exp_w1_2, exp_w3_2, exp_w2_2, final_g_2,
):
    x = first_block(
        x, c, ctx, c_ctx, w_ada, b_ada, norm1_gain, norm2_gain, w_in, mlstm_gate_bias,
        ret_decay_logit, w_ret_up, w_ml_up, w_out, w_ffn_in, w_ffn_out, final_gain,
    )
    return second_block(
        x, c_2, ctx_2, c_ctx_2, mod_w_2, mod_b_2, norm1_g_2, norm2_g_2, ev_w_in_2, ev_sink_2,
        ev_sgu_norm_g_2, ev_sgu_w_2, ev_sgu_b_2, ev_w_out_2, od_w_in_2, od_q_norm_g_2,
        od_w_uq_2, od_kv_norm_g_2, od_w_ukv_2, od_conv_w_2, od_w_out_2, router_w_2, exp_w1_2,
        exp_w3_2, exp_w2_2, final_g_2,
    )


_drawn_inputs = setup_inputs


def setup_inputs(seed=0):
    import zlib

    import numpy as np

    out = dict(_drawn_inputs(seed))
    spreads = {}
    factors = {'norm1_gain': 4.389,
     'norm2_gain': 7.098,
     'mod_b_2': 3.621,
     'norm2_g_2': 3.657,
     'ev_sink_2': 8.0,
     'ev_sgu_norm_g_2': 5.561,
     'ev_sgu_b_2': 2.891,
     'od_q_norm_g_2': 8.0,
     'od_w_uq_2': 2.916,
     'od_kv_norm_g_2': 8.0}
    for name, (base, spread) in spreads.items():
        noise = np.random.default_rng([zlib.crc32(name.encode()), seed]).standard_normal(out[name].shape)
        drawn = base * np.exp(spread * noise) if base else spread * noise
        out[name] = jnp.asarray(drawn.astype(out[name].dtype))
    for name, factor in factors.items():
        out[name] = (out[name] * factor).astype(out[name].dtype)
    return out
```

```python
from contextlib import ExitStack

import concourse.bass as bass
import numpy as np
from concourse import mybir

F32 = mybir.dt.float32
ACT = mybir.ActivationFunctionType
ALU = mybir.AluOpType
AX = mybir.AxisListType.X

P = 128
D = 1024
KD = D // P
N = 256
TC = N // P
HEADS = 4
FFN = 2816
KF = FFN // P
EPS = 1e-6
SLOTS = 6
E = 16
CAP = 32
FF = 1024
AH = 8
BIG = -1e30
DEPTH2 = 2
HD_SCALE = float(P) ** -0.5

C_ID, C_LE, C_GE, C_ONE, C_SWAP, C_SEL, C_IOTA, C_END = 0, 128, 256, 384, 512, 640, 644, 676
R_TS, R_ST, R_T1, R_TR, R_COS, R_SIN, R_SF, R_SB, R_END = 0, 256, 512, 768, 1024, 1280, 1536, 1538, 1540
M_COS, M_SIN, M_SWAP, M_HI, M_LO, M_END = 0, 256, 512, 640, 768, 896

V_BADA, V_BM = 0, 48
V_N1, V_N2, V_FG, V_C, V_CC = 144, 152, 160, 168, 176
V_M1, V_M2, V_FG2, V_C2, V_CC2 = 184, 200, 216, 224, 232
V_EVB, V_KV, V_QN, V_CONV, V_END = 240, 244, 246, 249, 261
V_TILES = -(-V_END // P)


def rope_table(per_head, heads):
    half = per_head // 2
    nf = per_head // 4
    inv = (10000.0 ** (-np.arange(nf, dtype=np.float32) / np.float32(nf))).astype(np.float32)
    rows = (np.arange(N) // 64).astype(np.float32)
    cols = (np.arange(N) % 64).astype(np.float32)
    ang = np.concatenate([rows[:, None] * inv, cols[:, None] * inv], axis=1).astype(np.float32)
    cos, sin = np.cos(ang).T.astype(np.float32), np.sin(ang).T.astype(np.float32)
    assert cos.shape[0] == half
    return (np.tile(np.concatenate([cos, cos]), (heads, 1)),
            np.tile(np.concatenate([-sin, sin]), (heads, 1)))


def swap_matrix(size, per_head, start=0):
    m = np.zeros((P, P), np.float32)
    half = per_head // 2
    for i in range(start, size):
        o = (i - start) % per_head
        m[i + half if o < half else i - half, i] = 1.0
    return m


def shape_constants():
    i = np.arange(P, dtype=np.float32)
    le = (i[:, None] <= i[None, :]).astype(np.float32)
    c = np.zeros((P, C_END), np.float32)
    c[:, C_ID:C_ID + P] = np.eye(P)
    c[:, C_LE:C_LE + P] = le
    c[:, C_GE:C_GE + P] = le.T
    c[:, C_ONE:C_ONE + P] = 1.0
    c[:, C_SWAP:C_SWAP + P] = swap_matrix(P, P)
    for g in range(4):
        c[32 * g:32 * g + 4, C_SEL:C_SEL + 4] = np.eye(4)
    c[:, C_IOTA:C_IOTA + CAP] = np.arange(1, CAP + 1)
    r = np.zeros((P, R_END), np.float32)
    t = np.arange(N, dtype=np.float32)
    r[:, R_TS:R_TS + N] = np.maximum(t[None, :] - i[:, None], 0)
    r[:, R_ST:R_ST + N] = np.maximum(i[:, None] + P - t[None, :], 0)
    r[:, R_T1:R_T1 + N] = t + 1
    r[:, R_TR:R_TR + N] = N - t
    r[:, R_COS:R_COS + N], r[:, R_SIN:R_SIN + N] = rope_table(P, 1)
    for s in range(TC):
        r[:, R_SF + s] = N - 1 - (i + P * s)
        r[:, R_SB + s] = i + P * s
    a = np.zeros((P, M_END), np.float32)
    a[:, M_COS:M_COS + N], a[:, M_SIN:M_SIN + N] = rope_table(64, 2)
    a[:, M_SWAP:M_SWAP + P] = swap_matrix(P, 64)
    a[:, M_HI:M_HI + P] = (1 - le.T) * BIG
    a[:, M_LO:M_LO + P] = (1 - le) * BIG
    b = np.zeros((P, M_END), np.float32)
    b[:, M_COS:M_COS + N] = 1.0
    b[64:96, M_COS:M_COS + N], b[64:96, M_SIN:M_SIN + N] = rope_table(32, 1)
    b[:, M_SWAP:M_SWAP + P] = swap_matrix(96, 32, 64)
    return {"const_all": c, "const_ret": r, "const_even": a, "const_odd": b}


class Jobs:

    def __init__(self, banks, filled, drained):
        self.banks, self.filled, self.drained = banks, filled, drained
        self.number = {}

    def new(self, job):
        assert job not in self.number, job
        self.number[job] = len(self.number)
        return self.at(job)[1]

    def at(self, job):
        n = self.number[job]
        return n % 8, n // 8 + 1

    def bank(self, job):
        return self.banks[:, self.at(job)[0], :]

    def is_free(self, job):
        b, turn = self.at(job)
        return self.drained[b], turn - 1

    def fills(self, job):
        return self.filled[self.at(job)[0]], 1

    def is_filled(self, job):
        b, turn = self.at(job)
        return self.filled[b], turn

    def is_drained(self, job):
        b, turn = self.at(job)
        return self.drained[b], turn


class Lane:

    def __init__(self, jobs, own, flag):
        self.jobs, self.own, self.flag = jobs, own, flag
        self.n, self.raised, self.last = 0, {}, None

    def steps(self):
        self.n += 1
        self.last = (self.own, self.n)
        return self.own, 1

    def raises(self, name):
        self.raised[name] = self.raised.get(name, 0) + 1
        self.last = (self.flag(name), self.raised[name])
        return self.flag(name), 1

    def frees(self, job):
        self.last = self.jobs.is_drained(job)
        return self.last[0], 1


def two_blocks(nc, t, out):
    with ExitStack() as ctx:
        def sb(name, cols):
            return ctx.enter_context(nc.sbuf_tensor(name, [P, cols], F32))

        semaphores = {}

        def flag(name):
            if name not in semaphores:
                semaphores[name] = ctx.enter_context(nc.semaphore(name))
            return semaphores[name]

        ring = ctx.enter_context(nc.sbuf_tensor("ring", [P, SLOTS, 4096], F32))
        arena = sb("arena", 16384)
        xT = ctx.enter_context(nc.sbuf_tensor("xT", [P, KD, N], F32))
        cT = ctx.enter_context(nc.sbuf_tensor("cT", [P, KD, N], F32))
        hT = ctx.enter_context(nc.sbuf_tensor("hT", [P, 2, KD, N], F32))
        const = sb("const", C_END)
        phase = sb("phase", R_END)
        vec = sb("vec", V_END)
        mod = ctx.enter_context(nc.sbuf_tensor("mod", [P, 3, 48, 2], F32))
        sil_c = ctx.enter_context(nc.sbuf_tensor("sil_c", [P, KD, 32], F32))
        modrow = sb("modrow", 512)
        small = sb("small", 232)
        banks = ctx.enter_context(nc.psum_tensor("banks", [P, 8, 512], F32))

        def carve(at, *shape):
            n = int(np.prod(shape))
            assert at + n <= 16384, (at, shape)
            v = arena[:, at:at + n]
            if len(shape) == 1:
                return v
            names = "abcd"[:len(shape)]
            return v.rearrange(f"p ({' '.join(names)}) -> p {' '.join(names)}",
                               **dict(zip(names[1:], shape[1:])))

        ident = const[:, C_ID:C_ID + P]
        tri_le, tri_ge = const[:, C_LE:C_LE + P], const[:, C_GE:C_GE + P]
        ones = const[:, C_ONE:C_ONE + P]
        swap128 = const[:, C_SWAP:C_SWAP + P]
        iota = const[:, C_IOTA:C_IOTA + CAP]
        hlat, hctx = hT[:, 0], hT[:, 1]
        eps = small[:, 0:1]
        lg = small[:, 8:16]
        sink = small[:, 16:24]
        nsm = small[:, 24:32]
        gate_bias = small[:, 32:33]
        mc = small[:, 34:35]
        total = small[:, 35:36]
        neg_mc = small[:, 36:37]
        mc_rep = small[:, 40:104]
        src_ret = small[:, 104:120].rearrange("p (d s h) -> p d s h", d=2, s=2)
        gainA = small[:, 120:136].rearrange("p (s k) -> p s k", s=2)
        segs = small[:, 136:152]
        dn = small[:, 152:160].rearrange("p (a d) -> p a d", a=4)
        att = small[:, 160:192].rearrange("p (a b) -> p a b", a=8)
        lnst = small[:, 192:216].rearrange("p (c a) -> p c a", a=6)
        rt4 = small[:, 216:224].rearrange("p (a b) -> p a b", a=2)
        mx8 = small[:, 224:232]

        k_src = [[carve(1024 * (2 * m + d), TC, 512) for d in range(2)] for m in range(2)]
        vc_r = carve(4096, TC, 512)
        vc_m = carve(5120, TC, HEADS, P + 1)
        rqT, mqT = carve(0, HEADS, N), carve(1024, HEADS, N)
        rg, mo = carve(2048, TC, 512), carve(3072, TC, 512)
        decay = carve(4096, HEADS, 512)
        rkT, mkT = carve(6160, HEADS, N), carve(7184, HEADS, N)
        rv, mv = carve(8208, TC, 512), carve(9232, TC, HEADS, P + 1)
        s_ret = carve(10264, 2, HEADS, P)
        s_ml = carve(11288, 2, HEADS, P + 1)
        G0 = 12320
        row_c, row_g, row_e = (carve(G0 + 256 * i, 256) for i in range(3))
        rI, rF, rL, rB, rG, rC, rE, zero = (carve(G0 + 768 + 256 * i, 256) for i in range(8))
        mg_raw = carve(G0 + 2816, KD, 16)
        mg_w = carve(G0 + 2944, KD, 2, 64)
        gcols = ctx.enter_context(nc.sbuf_tensor("gcols", [P, 4, 32 + HEADS], F32))
        wcols = ctx.enter_context(nc.sbuf_tensor("wcols", [P, TC, 32 + HEADS], F32))
        p_ret = carve(G0 + 768, 2, 512)
        q_ret = carve(G0 + 1792, 2, 2, N)
        p_ml = carve(G0 + 768, 2, 2, 384)
        q_ml = carve(G0 + 2304, 2, 2, N)
        ret = cT[:, 0:4, :].rearrange("p a b -> p (a b)").rearrange("p (c n) -> p c n", c=TC)
        ml = cT[:, 4:8, :].rearrange("p a b -> p (a b)").rearrange("p (c n) -> p c n", c=TC)
        yT = hctx
        sig_r, sig_m = carve(0, KD, N), carve(2048, KD, N)
        merged = carve(4096, KD, N)
        f_g = carve(6160, KF, N)
        f_sil = carve(12320, 2, N)
        stage = [carve(0, TC, D), carve(2048, TC, D)]
        vrows = carve(4096, V_TILES, P)

        e_k, e_q, e_v = carve(0, 512), carve(512, 4, 512), carve(2560, 4, P)
        e_u, e_w = carve(3072, 4, 512), carve(5120, 4, 512)
        e_o = carve(7168, 4, 512)
        e_cat = carve(9216, KD, 512)
        e_p, e_pT = carve(13312, 2, 512), carve(14336, 2, 4, P)
        e_gain = carve(15360, 512)
        e_ws = carve(15872, 4, P)
        ws_raw = carve(12832, 4, P)
        stage2 = hctx.rearrange("p k n -> p (k n)").rearrange("p (c d) -> p c d", c=TC)
        o_k, o_q, o_v = carve(0, AH, 512), carve(4096, AH, N), carve(6144, 4, 512)
        o_ckv, o_cq, o_sq = carve(8192, 2, 512), carve(9216, 3, N), carve(9984, 2, 512)
        o_kr = carve(11008, 512)
        o_gb, o_gc, o_hh = (carve(11520 + 1024 * i, 4, N) for i in range(3))
        o_o = carve(8192, TC, 512)
        o_p, o_pT = carve(9216, 2, 512), carve(10240, 2, 4, P)
        o_cat = hctx

        tokens_of = carve(8192, 4, D)
        y_of = [carve(8192, 4, D), hT[:].rearrange("p a b c -> p (a b c)").rearrange("p (g n) -> p g n", g=4)]
        GT = [carve(12288, 4, N), carve(13312, 4, N)]
        x_g = carve(14336, 512)
        x_gT = carve(14848, 512)
        x_cur = carve(15360, 2, 512)
        x_sil = modrow
        sel_of = [hT[:].rearrange("p a b c -> p (a b c)")[:, 1024 * s:1024 * s + 1024]
                  .rearrange("p (c n) -> p c n", c=TC) for s in range(4)]
        logit = carve(14336, 64)
        aff = carve(14400, 2, TC, E)
        affp = carve(14464, TC, 48)
        aw = carve(14560, N)
        mk = carve(14816, N)
        mt = carve(15072, TC, 48)
        pm = carve(15168, TC, 48)
        rws = [phase[:, 1024 + P * l:1024 + P * l + P].rearrange("p (k e) -> p k e", e=E) for l in range(DEPTH2)]

        blocks = []

        def rows_of(w, c0, width):
            return w.rearrange("(k p) n -> p k n", p=P)[:, :, c0:c0 + width]

        def block_of(name, *parts):
            blocks.append((name, parts))

        def w8(name, w, c0, width):
            block_of(name, (0, (KD, width), rows_of(w, c0, width)))

        ada, m_w = t["w_ada"][0], t["mod_w_2"]
        w_in = t["w_in"][0]
        offs = {"rq": 0, "rk": 512, "rv": 1024, "rg": 1536, "mq": 2048, "mk": 2560, "mv": 3072, "mo": 3584}
        for b in range(4):
            w8(f"a{b}", ada, 512 * b, 512)
        for n in ("rk", "rv", "mk", "mv", "rq", "mq", "rg", "mo"):
            w8(n, w_in, offs[n], 512)
        for b in range(8):
            w8(f"a{4 + b}", ada, 512 * (4 + b), 512)
        for b in range(4):
            w8(f"bg{b}", w_in, 4112 + 512 * b, 512)
        block_of("r_up", (0, (4, D), t["w_ret_up"][0].rearrange("(k p) n -> p k n", p=P)))
        block_of("m_up", (0, (4, D), t["w_ml_up"][0].rearrange("(k p) n -> p k n", p=P)))
        for b in range(2):
            w8(f"wo{b}", t["w_out"][0], 512 * b, 512)
        w_f = t["w_ffn_in"][0]
        for b in range(KF // 2):
            block_of(f"fi{b}", *[(256 * s, (KD, 512), rows_of(w_f, FFN * s + 256 * b, 256)) for s in range(2)])
            w8(f"b{b}", m_w[0], 512 * b, 512)
        w8("b11", m_w[0], 512 * 11, 512)
        for b in range(KD):
            block_of(f"fo{b}", (0, (KF, P), rows_of(t["w_ffn_out"][0], P * b, P)))
        ev = t["ev_w_in_2"][0]
        w8("ekv", ev, 0, 256)
        w8("eq", ev, 256, 512)
        w8("eu", ev, 768, 512)
        w8("ew", ev, 1280, 512)
        for b in range(12):
            w8(f"c{b}", m_w[1], 512 * b, 512)
        for b in range(2):
            w8(f"eo{b}", t["ev_w_out_2"][0], 512 * b, 512)
        first_experts = [len(blocks)]
        blocks += [(f"x0_{i}", None) for i in range(6 * E)]
        od = t["od_w_in_2"][0]
        w8("ock", od, 0, 288)
        w8("ocq", od, 288, 384)
        w8("ogb", od, 672, 512)
        block_of("ukv", (0, (2, D), t["od_w_ukv_2"][0].rearrange("(k p) n -> p k n", p=P)))
        block_of("uq", (0, (3, 768), t["od_w_uq_2"][0].rearrange("(k p) n -> p k n", p=P)))
        w8("ogc", od, 1184, 512)
        w8("ohh", od, 1696, 512)
        for b in range(2):
            w8(f"oo{b}", t["od_w_out_2"][0], 512 * b, 512)
        first_experts.append(len(blocks))
        blocks += [(f"x1_{i}", None) for i in range(6 * E)]
        index = {name: i for i, (name, _) in enumerate(blocks)}
        landed, sums = {}, [0] * SLOTS
        for i, (name, parts) in enumerate(blocks):
            sums[i % SLOTS] += 16 * (len(parts) if parts else 1)
            landed[name] = sums[i % SLOTS]
        last_job = {}

        filled = [flag(f"psum_filled_{b}") for b in range(8)]
        drained = [flag(f"psum_drained_{b}") for b in range(8)]
        jobs = Jobs(banks, filled, drained)
        arrived = [flag(f"weights_in_slot_{s}") for s in range(SLOTS)]
        XJ = 7

        def vector_rows():
            flat = lambda a: a.rearrange(" ".join("abcd"[:len(a.shape)]) + " -> (" + " ".join("abcd"[:len(a.shape)]) + ")")
            for at, a in ((V_BADA, t["b_ada"]), (V_BM, t["mod_b_2"]), (V_N1, t["norm1_gain"]),
                          (V_N2, t["norm2_gain"]), (V_FG, t["final_gain"]), (V_C, t["c"]), (V_CC, t["c_ctx"]),
                          (V_M1, t["norm1_g_2"]), (V_M2, t["norm2_g_2"]), (V_FG2, t["final_g_2"]),
                          (V_C2, t["c_2"]), (V_CC2, t["c_ctx_2"]), (V_EVB, t["ev_sgu_b_2"]),
                          (V_KV, t["od_kv_norm_g_2"]), (V_QN, t["od_q_norm_g_2"]), (V_CONV, t["od_conv_w_2"])):
                a = (flat(a) if len(a.shape) > 1 else a).rearrange("(r p) -> r p", p=P)
                n, done = a.shape[0], 0
                while done < n:
                    row = at + done
                    m = min(n - done, P - row % P)
                    yield row // P, row % P, a[done:done + m, :]
                    done += m

        vector_loads = list(vector_rows())
        block = ctx.enter_context(nc.Block())

        A_TILES = [(0, c, h) for c in range(TC) for h in range(AH)]
        C_TILES = [(1, c, h) for c in range(TC) for h in range(AH)]
        EVEN_TILES, ODD_TILES = A_TILES + C_TILES, A_TILES
        CONV_AT = {0: ("ohh", 0), 2: ("ohh", 1)}
        MODL = {"a": 0, "b": 1, "c": 2}

        @block.tensor
        def _(eng):
            mm = nc.tensor.matmul

            def arrives(name):
                return arrived[index[name] % SLOTS], landed[name]

            def slot(name, width):
                return ring[:, index[name] % SLOTS, 0:4096 // width * width].rearrange("p (k n) -> p k n", n=width)

            def used(name, job):
                last_job[name] = job

            def turn(job, pieces):
                o = jobs.bank(job)
                for at, src in pieces:
                    k = src.shape[0]
                    m = src.shape[1]
                    ins = nc.tensor.transpose(o[0:m, at:at + k], src, ident[0:k, 0:k])
                return ins

            def mod_rows(l, b):
                eng.wait_ge(*arrives(f"{l}{b}"))
                w = slot(f"{l}{b}", 512)
                job = f"mod_{l}{b}"
                if jobs.new(job) > 1:
                    eng.wait_ge(*jobs.is_free(job))
                o = jobs.bank(job)
                for r in range(2):
                    for g in range(4):
                        k = 4 * r + g
                        ins = mm(o[32 * g:32 * g + 32, :], sil_c[:, k, :], w[:, k, :],
                                 start=(r == 0), stop=(r == 1), skip_group_check=True)
                ins.then_inc(*jobs.fills(job))
                used(f"{l}{b}", job)

            def mod_cols(l, b):
                eng.wait_ge(*jobs.is_drained(f"mod_{l}{b}"))
                job = f"modT_{l}{b}"
                if jobs.new(job) > 1:
                    eng.wait_ge(*jobs.is_free(job))
                o = jobs.bank(job)
                c0 = C_SEL + (0 if l == "a" else 2)
                for c in range(4):
                    ins = mm(o[:, 2 * c:2 * c + 2], modrow[:, P * c:P * c + P], const[:, c0:c0 + 2],
                             start=True, stop=True)
                ins.then_inc(*jobs.fills(job))

            pending = []

            def mods(l, b):
                if pending:
                    mod_cols(*pending.pop())
                mod_rows(l, b)
                pending.append((l, b))

            def mods_end():
                while pending:
                    mod_cols(*pending.pop())

            def sum_squares(tag, s):
                if jobs.new(f"{tag}_ss{s}") > 1:
                    eng.wait_ge(*jobs.is_free(f"{tag}_ss{s}"))
                o = jobs.bank(f"{tag}_ss{s}")
                for k in range(KD):
                    if k % 2 == 0:
                        sum_squares.n += 1
                        eng.wait_ge(flag("squares"), sum_squares.n)
                    ins = mm(o[:, 0:N], ones, hT[:, s, k, :], start=(k == 0), stop=(k == KD - 1))
                ins.then_inc(*jobs.fills(f"{tag}_ss{s}"))
            sum_squares.n = 0

            def project(pieces):
                for dst, terms in pieces:
                    for i, (a, b) in enumerate(terms):
                        ins = mm(dst, a, b, start=(i == 0), stop=(i == len(terms) - 1))
                return ins

            def token_major(o, s, c, w):
                return [(o[:, :], [(hT[:, s, k, P * c:P * c + P], w[:, k, :]) for k in range(KD)])]

            eng.wait_ge(flag("consts_in"), 16)
            eng.wait_ge(flag("vectors_in"), 16 * len(vector_loads))
            for i in range(V_TILES):
                n = min(P, V_END - P * i)
                if jobs.new(f"vec{i}") > 1:
                    eng.wait_ge(*jobs.is_free(f"vec{i}"))
                turn(f"vec{i}", [(0, vrows[0:n, i, :])]).then_inc(*jobs.fills(f"vec{i}"))
            eng.wait_ge(flag("tokens_in"), 32)
            for s in range(2):
                for a in range(4):
                    if jobs.new(f"xt{s}{a}") > 1:
                        eng.wait_ge(*jobs.is_free(f"xt{s}{a}"))
                    turn(f"xt{s}{a}", [(256 * b + P * c, stage[s][:, c, P * (2 * a + b):P * (2 * a + b) + P])
                                       for b in range(2) for c in range(TC)]).then_inc(*jobs.fills(f"xt{s}{a}"))
            eng.wait_ge(flag("silu_c"), 1)
            for s in (1, 0):
                sum_squares("n1", s)
            for b in range(4):
                mods("a", b)
            mods_end()
            eng.wait_ge(flag("gate_weights"), 1)
            for s in (1, 0):
                eng.wait_ge(flag(f"h1_{s}"), 1)
                eng.wait_ge(flag(f"h1_{s}_v"), 1)
                if jobs.new(f"gates{s}") > 1:
                    eng.wait_ge(*jobs.is_free(f"gates{s}"))
                o = jobs.bank(f"gates{s}")
                project([(o[:, 0:N], [(mg_w[:, k, :, :], hT[:, s, k, :]) for k in range(KD)])]).then_inc(*jobs.fills(f"gates{s}"))

            for n in ("rk", "rv", "mk", "mv"):
                eng.wait_ge(*arrives(n))
                w = slot(n, 512)
                for c in range(TC):
                    job = f"c_{n}{c}"
                    if jobs.new(job) > 1:
                        eng.wait_ge(*jobs.is_free(job))
                    o = jobs.bank(job)
                    project(token_major(o, 1, c, w)).then_inc(*jobs.fills(job))
                for c in range(TC):
                    job = f"x_{n}{c}"
                    if jobs.new(job) > 1:
                        eng.wait_ge(*jobs.is_free(job))
                    o = jobs.bank(job)
                    if n[1] == "v":
                        project(token_major(o, 0, c, w)).then_inc(*jobs.fills(job))
                    else:
                        project([(o[:, N * j:N * j + N],
                                          [(w[:, k, P * (2 * c + j):P * (2 * c + j) + P], hlat[:, k, :])
                                           for k in range(KD)]) for j in range(2)]).then_inc(*jobs.fills(job))
                used(n, job)
                if n == "rk":
                    eng.wait_ge(flag("source_rows"), 1)
                    if jobs.new("src_cols") > 1:
                        eng.wait_ge(*jobs.is_free("src_cols"))
                    turn("src_cols", [(64 * c, carve(G0 + 768 + 256 * 6, 256)[0:64, P * c:P * c + P]) for c in range(TC)]).then_inc(*jobs.fills("src_cols"))
                    eng.wait_ge(flag("rows_done"), 1)
                    if jobs.new("gate_cols") > 1:
                        eng.wait_ge(*jobs.is_free("gate_cols"))
                    turn("gate_cols", [(64 * (2 * y + c), r[0:64, P * c:P * c + P])
                                       for y, r in enumerate((row_g, row_e)) for c in range(TC)]).then_inc(*jobs.fills("gate_cols"))
                    if jobs.new("mc_rep") > 1:
                        eng.wait_ge(*jobs.is_free("mc_rep"))
                    o = jobs.bank("mc_rep")
                    mm(o[:, 0:64], mc[0:64, :].broadcast_to((64, P)), ident[0:64, 0:64], start=True, stop=True).then_inc(*jobs.fills("mc_rep"))
            for n in ("c_rk1", "c_rv1"):
                eng.wait_ge(*jobs.is_drained(n))
            for d in range(2):
                job = f"s_ret{d}"
                if jobs.new(job) > 1:
                    eng.wait_ge(*jobs.is_free(job))
                o = jobs.bank(job)
                project([(o[:, P * h:P * h + P],
                                  [(k_src[0][d][:, c, P * h:P * h + P], vc_r[:, c, P * h:P * h + P])
                                   for c in range(TC)]) for h in range(HEADS)]).then_inc(*jobs.fills(job))
            for n in ("c_mk1", "c_mv1"):
                eng.wait_ge(*jobs.is_drained(n))
            for d in range(2):
                for a in range(2):
                    job = f"s_ml{d}{a}"
                    if jobs.new(job) > 1:
                        eng.wait_ge(*jobs.is_free(job))
                    o = jobs.bank(job)
                    project([(o[:, 129 * j:129 * j + 129],
                                      [(k_src[1][d][:, c, P * h:P * h + P], vc_m[:, c, h, :])
                                       for c in range(TC)]) for j, h in enumerate((2 * a, 2 * a + 1))]).then_inc(*jobs.fills(job))
            for n in ("rq", "mq", "rg", "mo"):
                if n == "rg":
                    for m, x in (("rk", rkT), ("rq", rqT)):
                        for a in range(2):
                            eng.wait_ge(*jobs.is_drained(f"x_{m}{a}"))
                            job = f"swap_{m}{a}"
                            if jobs.new(job) > 1:
                                eng.wait_ge(*jobs.is_free(job))
                            o = jobs.bank(job)
                            mm(o[:, :], swap128, x[:, 2 * a:2 * a + 2, :].rearrange("p a n -> p (a n)"),
                                    start=True, stop=True).then_inc(*jobs.fills(job))
                eng.wait_ge(*arrives(n))
                w = slot(n, 512)
                for c in range(TC):
                    job = f"x_{n}{c}"
                    if jobs.new(job) > 1:
                        eng.wait_ge(*jobs.is_free(job))
                    o = jobs.bank(job)
                    if n in ("rg", "mo"):
                        project(token_major(o, 0, c, w)).then_inc(*jobs.fills(job))
                    else:
                        project([(o[:, N * j:N * j + N],
                                          [(w[:, k, P * (2 * c + j):P * (2 * c + j) + P], hlat[:, k, :])
                                           for k in range(KD)]) for j in range(2)]).then_inc(*jobs.fills(job))
                used(n, job)
            eng.wait_ge(flag("rope_ret"), 4)

            def ret_scores(h):
                job = f"rs{h}"
                if jobs.new(job) > 1:
                    eng.wait_ge(*jobs.is_free(job))
                o = jobs.bank(job)
                project([(o[:, N * s:N * s + N], [(rkT[:, h, P * s:P * s + P], rqT[:, h, :])])
                                 for s in range(TC)]).then_inc(*jobs.fills(job))

            eng.wait_ge(*jobs.is_drained("s_ret1"))
            ret_scores(0)
            for h in range(HEADS):
                if h + 1 < HEADS:
                    ret_scores(h + 1)
                mods("a", 4 + h)
                eng.wait_ge(flag("ret_q"), 2 * h + 2)
                eng.wait_ge(*jobs.is_drained(f"rs{h}"))
                job = f"ro{h}"
                if jobs.new(job) > 1:
                    eng.wait_ge(*jobs.is_free(job))
                o = jobs.bank(job)
                project([(o[:, P * c:P * c + P],
                                  [(p_ret[:, h % 2, N * s + P * c:N * s + P * c + P], rv[:, s, P * h:P * h + P])
                                   for s in range(TC)] +
                                  [(q_ret[:, h % 2, d, P * c:P * c + P], s_ret[:, d, h, :]) for d in range(2)])
                                 for c in range(TC)]).then_inc(*jobs.fills(job))
            eng.wait_ge(*jobs.is_drained("s_ml11"))

            def ml_scores(h):
                for d in range(2):
                    job = f"cr{h}{d}"
                    if jobs.new(job) > 1:
                        eng.wait_ge(*jobs.is_free(job))
                    o = jobs.bank(job)
                    r = 32 * d + h
                    mm(o[:, 0:N], ident[0:64, r:r + 1].broadcast_to((64, P)), row_c[0:64, :],
                            start=True, stop=True).then_inc(*jobs.fills(job))
                job = f"ms{h}"
                if jobs.new(job) > 1:
                    eng.wait_ge(*jobs.is_free(job))
                o = jobs.bank(job)
                project([(o[:, N * s:N * s + N], [(mkT[:, h, P * s:P * s + P], mqT[:, h, :])])
                                 for s in range(TC)]).then_inc(*jobs.fills(job))

            ml_scores(0)
            for h in range(HEADS):
                mods("a", 8 + h)
                eng.wait_ge(flag("ml_q"), 2 * h + 2)
                eng.wait_ge(*jobs.is_drained(f"ms{h}"))
                for c in range(TC):
                    job = f"mo{h}{c}"
                    if jobs.new(job) > 1:
                        eng.wait_ge(*jobs.is_free(job))
                    o = jobs.bank(job)
                    pieces = []
                    for d in range(2):
                        take = {(0, 0): [(0, 0)], (0, 1): [(1, 0), (2, 1)], (1, 0): [(0, 0), (1, 1)], (1, 1): [(2, 1)]}
                        pieces.append((o[:, 129 * d:129 * d + 129],
                                       [(p_ml[:, h % 2, d, P * b:P * b + P], mv[:, s, h, :]) for b, s in take[d, c]] +
                                       [(q_ml[:, h % 2, d, P * c:P * c + P], s_ml[:, d, h, :])]))
                    project(pieces).then_inc(*jobs.fills(job))
                if h + 1 < HEADS:
                    ml_scores(h + 1)
            mods_end()
            for b in range(4):
                eng.wait_ge(*arrives(f"bg{b}"))
                w = slot(f"bg{b}", 512)
                for a in range(2):
                    job = f"bg{b}{a}"
                    if jobs.new(job) > 1:
                        eng.wait_ge(*jobs.is_free(job))
                    o = jobs.bank(job)
                    project([(o[:, N * j:N * j + N],
                                      [(w[:, k, P * (2 * a + j):P * (2 * a + j) + P], hlat[:, k, :])
                                       for k in range(KD)]) for j in range(2)]).then_inc(*jobs.fills(job))
                used(f"bg{b}", job)
            for m, y in enumerate((ret, ml)):
                eng.wait_ge(flag("y_normed"), m + 1)
                for a in range(2):
                    if jobs.new(f"yT{m}{a}") > 1:
                        eng.wait_ge(*jobs.is_free(f"yT{m}{a}"))
                    turn(f"yT{m}{a}", [(N * j + P * c, y[:, c, P * (2 * a + j):P * (2 * a + j) + P])
                                       for j in range(2) for c in range(TC)]).then_inc(*jobs.fills(f"yT{m}{a}"))
            eng.wait_ge(*arrives("r_up"))
            eng.wait_ge(*arrives("m_up"))
            ups = [slot("r_up", D), slot("m_up", D)]
            eng.wait_ge(*jobs.is_drained("yT01"))
            eng.wait_ge(*jobs.is_drained("yT11"))
            for n in range(KD):
                job = f"up{n}"
                if jobs.new(job) > 1:
                    eng.wait_ge(*jobs.is_free(job))
                o = jobs.bank(job)
                project([(o[:, N * m:N * m + N],
                                  [(ups[m][:, k, P * n:P * n + P], yT[:, 4 * m + k, :]) for k in range(4)])
                                 for m in range(2)]).then_inc(*jobs.fills(job))
            used("r_up", job)
            used("m_up", job)
            eng.wait_ge(flag("merged"), KD)
            for b in range(2):
                eng.wait_ge(*arrives(f"wo{b}"))
                w = slot(f"wo{b}", 512)
                for a in range(2):
                    job = f"wo{2 * b + a}"
                    if jobs.new(job) > 1:
                        eng.wait_ge(*jobs.is_free(job))
                    o = jobs.bank(job)
                    project([(o[:, N * j:N * j + N],
                                      [(w[:, k, P * (2 * a + j):P * (2 * a + j) + P], merged[:, k, :])
                                       for k in range(KD)]) for j in range(2)]).then_inc(*jobs.fills(job))
                used(f"wo{b}", job)
            sum_squares("n2", 0)
            eng.wait_ge(flag("h2_0"), 1)
            eng.wait_ge(flag("h2_0_v"), 1)
            for b in range(KF // 2):
                eng.wait_ge(*arrives(f"fi{b}"))
                w = slot(f"fi{b}", 512)
                for a in range(2):
                    job = f"fi{2 * b + a}"
                    if jobs.new(job) > 1:
                        eng.wait_ge(*jobs.is_free(job))
                    o = jobs.bank(job)
                    project([(o[:, N * m:N * m + N],
                                      [(w[:, k, 256 * m + P * a:256 * m + P * a + P], hlat[:, k, :])
                                       for k in range(KD)]) for m in range(2)]).then_inc(*jobs.fills(job))
                used(f"fi{b}", job)
                mods("b", b)
            mods("b", 11)
            eng.wait_ge(flag("tokens_in"), 48)
            for a in range(4):
                if jobs.new(f"yt{a}") > 1:
                    eng.wait_ge(*jobs.is_free(f"yt{a}"))
                turn(f"yt{a}", [(256 * b + P * c, stage2[:, c, P * (2 * a + b):P * (2 * a + b) + P])
                                for b in range(2) for c in range(TC)]).then_inc(*jobs.fills(f"yt{a}"))
            eng.wait_ge(*jobs.is_drained(f"fi{KF - 1}"))
            for b in range(KD):
                eng.wait_ge(*arrives(f"fo{b}"))
                w = slot(f"fo{b}", P)
                job = f"fo{b}"
                if jobs.new(job) > 1:
                    eng.wait_ge(*jobs.is_free(job))
                o = jobs.bank(job)
                project([(o[:, 0:N], [(w[:, k, :], f_g[:, k, :]) for k in range(KF)])]).then_inc(*jobs.fills(job))
                used(f"fo{b}", job)
                mods_end()
                if b == 3:
                    sum_squares("e1", 1)
            sum_squares("nf", 0)

            def conv_inputs(n, a):
                eng.wait_ge(*arrives(n))
                w = slot(n, 512)
                job = f"{n}{a}"
                if jobs.new(job) > 1:
                    eng.wait_ge(*jobs.is_free(job))
                o = jobs.bank(job)
                project([(o[:, N * j:N * j + N],
                          [(w[:, k, P * (2 * a + j):P * (2 * a + j) + P], hlat[:, k, :])
                           for k in range(KD)]) for j in range(2)]).then_inc(*jobs.fills(job))
                used(n, job)

            def attention(tag, tiles, scores, values):
                T = len(tiles)
                for i in range(T + 3):
                    if i < T:
                        s, c, h = tiles[i]
                        job = f"{tag}_s{i}"
                        if jobs.new(job) > 1:
                            eng.wait_ge(*jobs.is_free(job))
                        o = jobs.bank(job)
                        a, b = scores(s, c, h)
                        mm(o[:, 0:b.shape[-1]], a, b, start=True, stop=True).then_inc(*jobs.fills(job))
                    if 2 <= i < T + 2:
                        j = i - 2
                        kc = 4 if tiles[j][0] == 0 else 2
                        eng.wait_ge(*jobs.is_drained(f"{tag}_s{j}"))
                        if jobs.new(f"{tag}_t{j}") > 1:
                            eng.wait_ge(*jobs.is_free(f"{tag}_t{j}"))
                        turn(f"{tag}_t{j}", [(P * q, att_p[:, j % 2, P * q:P * q + P]) for q in range(kc)]).then_inc(*jobs.fills(f"{tag}_t{j}"))
                    if i >= 3:
                        j = i - 3
                        s, c, h = tiles[j]
                        eng.wait_ge(*jobs.is_drained(f"{tag}_t{j}"))
                        job = f"{tag}_o{j}"
                        if jobs.new(job) > 1:
                            eng.wait_ge(*jobs.is_free(job))
                        o = jobs.bank(job)
                        kc = range(4) if s == 0 else range(2)
                        project([(o[:, 0:64], [(att_pT[:, j % 2, q, :], values(s, q, h)) for q in kc])]).then_inc(*jobs.fills(job))
                    if tag == "ea" and i % 3 == 1:
                        mods("c", i // 3)
                    if tag == "oa" and i in CONV_AT:
                        conv_inputs(*CONV_AT[i])
                mods_end()

            sum_squares("e1", 0)
            eng.wait_ge(flag("h3_0"), 1)
            eng.wait_ge(flag("h3_0_v"), 1)
            eng.wait_ge(flag("h3_1"), 1)
            eng.wait_ge(flag("h3_1_v"), 1)
            eng.wait_ge(*arrives("ekv"))
            w = slot("ekv", 256)
            if jobs.new("e_k") > 1:
                eng.wait_ge(*jobs.is_free("e_k"))
            o = jobs.bank("e_k")
            project([(o[:, :], [(w[:, k, 0:P], hT[:, :, k, :]) for k in range(KD)])]).then_inc(*jobs.fills("e_k"))
            if jobs.new("e_v") > 1:
                eng.wait_ge(*jobs.is_free("e_v"))
            o = jobs.bank("e_v")
            project([(o[:, P * (2 * s + c):P * (2 * s + c) + P],
                                [(hT[:, s, k, P * c:P * c + P], w[:, k, P:2 * P]) for k in range(KD)])
                               for s in range(2) for c in range(TC)]).then_inc(*jobs.fills("e_v"))
            used("ekv", "e_v")
            eng.wait_ge(*arrives("eq"))
            w = slot("eq", 512)
            for j in range(4):
                job = f"e_q{j}"
                if jobs.new(job) > 1:
                    eng.wait_ge(*jobs.is_free(job))
                o = jobs.bank(job)
                for k in range(KD):
                    for half in range(2):
                        ins = mm(o[64 * half:64 * half + 64, :], w[:, k, 64 * (j + 4 * half):64 * (j + 4 * half) + 64],
                                 hT[:, :, k, :], start=(k == 0), stop=(k == KD - 1), skip_group_check=True)
                ins.then_inc(*jobs.fills(job))
            used("eq", job)
            eng.wait_ge(flag("ws_in"), 16)
            if jobs.new("e_ws") > 1:
                eng.wait_ge(*jobs.is_free("e_ws"))
            turn("e_ws", [(P * g, ws_raw[:, g, :]) for g in range(4)]).then_inc(*jobs.fills("e_ws"))
            for n in ("eu", "ew"):
                if n == "ew":
                    eng.wait_ge(flag("even_consts_in"), 16)
                    swapA = phase[:, M_SWAP:M_SWAP + P]
                    eng.wait_ge(*jobs.is_drained("e_k"))
                    if jobs.new("esw0") > 1:
                        eng.wait_ge(*jobs.is_free("esw0"))
                    o = jobs.bank("esw0")
                    mm(o[:, 0:N], swapA, e_k[:, 0:N], start=True, stop=True).then_inc(*jobs.fills("esw0"))
                    for a in range(2):
                        eng.wait_ge(*jobs.is_drained(f"e_q{2 * a + 1}"))
                        if jobs.new(f"esw{a + 1}") > 1:
                            eng.wait_ge(*jobs.is_free(f"esw{a + 1}"))
                        o = jobs.bank(f"esw{a + 1}")
                        mm(o[:, :], swapA, e_q[:, 2 * a:2 * a + 2, 0:N], start=True, stop=True).then_inc(*jobs.fills(f"esw{a + 1}"))
                eng.wait_ge(*arrives(n))
                w = slot(n, 512)
                for c in range(4):
                    job = f"{n}{c}"
                    if jobs.new(job) > 1:
                        eng.wait_ge(*jobs.is_free(job))
                    o = jobs.bank(job)
                    project(token_major(o, c // 2, c % 2, w)).then_inc(*jobs.fills(job))
                used(n, job)
            eng.wait_ge(flag("rope_even"), 3)
            eng.wait_ge(*jobs.is_drained("e_v"))
            att_p, att_pT = e_p, e_pT

            def e_scores(s, c, h):
                r = 64 * (h // 4)
                return (e_q[r:r + 64, h % 4, N * s + P * c:N * s + P * c + P],
                        e_k[r:r + 64, N * s:512])

            attention("ea", EVEN_TILES, e_scores,
                      lambda s, q, h: e_v[:, 2 * s + q, 64 * (h // 4):64 * (h // 4) + 64])
            eng.wait_ge(flag("sgu_v"), 4)
            eng.wait_ge(*jobs.is_drained("e_ws"))
            for c in range(4):
                job = f"em{c}"
                if jobs.new(job) > 1:
                    eng.wait_ge(*jobs.is_free(job))
                o = jobs.bank(job)
                project([(o[:, P * g:P * g + P], [(e_ws[:, g, :], e_w[:, c, P * g:P * g + P])])
                                 for g in range(4)]).then_inc(*jobs.fills(job))
            for c in range(4):
                eng.wait_ge(flag("att_out_even"), 1)
                if jobs.new(f"ect{c}0") > 1:
                    eng.wait_ge(*jobs.is_free(f"ect{c}0"))
                turn(f"ect{c}0", [(P * j, e_o[:, c, P * j:P * j + P]) for j in range(4)]).then_inc(*jobs.fills(f"ect{c}0"))
                eng.wait_ge(*jobs.is_drained(f"em{c}"))
                if jobs.new(f"ect{c}1") > 1:
                    eng.wait_ge(*jobs.is_free(f"ect{c}1"))
                turn(f"ect{c}1", [(P * j, e_u[:, c, P * j:P * j + P]) for j in range(4)]).then_inc(*jobs.fills(f"ect{c}1"))
            for c in range(4):
                for y in range(2):
                    eng.wait_ge(*jobs.is_drained(f"ect{c}{y}"))
            for b in range(2):
                eng.wait_ge(*arrives(f"eo{b}"))
                w = slot(f"eo{b}", 512)
                for a in range(4):
                    job = f"eo{4 * b + a}"
                    if jobs.new(job) > 1:
                        eng.wait_ge(*jobs.is_free(job))
                    o = jobs.bank(job)
                    project([(o[:, :], [(w[:, k, P * a:P * a + P], e_cat[:, k, :]) for k in range(KD)])]).then_inc(*jobs.fills(job))
                used(f"eo{b}", job)

            def routed(l, streams, hname):
                for s in streams:
                    sum_squares(f"r{l}", s)
                for s in streams:
                    eng.wait_ge(flag(f"{hname}_{s}"), 1)
                    eng.wait_ge(flag(f"{hname}_{s}_v"), 1)
                eng.wait_ge(flag("router_in"), 32)
                job = f"rt{l}"
                if jobs.new(job) > 1:
                    eng.wait_ge(*jobs.is_free(job))
                o = jobs.bank(job)
                project([(o[:, E * (2 * s + c):E * (2 * s + c) + E],
                                  [(hT[:, s, k, P * c:P * c + P], rws[l][:, k, :]) for k in range(KD)])
                                 for s in streams for c in range(TC)]).then_inc(*jobs.fills(job))
                for s in streams:
                    for c in range(TC):
                        for a in range(2):
                            if jobs.new(f"th{l}{s}{c}{a}") > 1:
                                eng.wait_ge(*jobs.is_free(f"th{l}{s}{c}{a}"))
                            turn(f"th{l}{s}{c}{a}", [(P * j, hT[:, s, 4 * a + j, P * c:P * c + P]) for j in range(4)]).then_inc(*jobs.fills(f"th{l}{s}{c}{a}"))
                eng.wait_ge(flag("affinities"), l + 1)
                if jobs.new(f"at{l}") > 1:
                    eng.wait_ge(*jobs.is_free(f"at{l}"))
                turn(f"at{l}", [(P * c, affp[:, c, :]) for c in range(TC)]).then_inc(*jobs.fills(f"at{l}"))
                eng.wait_ge(flag("chosen"), l + 1)
                if jobs.new(f"mk{l}") > 1:
                    eng.wait_ge(*jobs.is_free(f"mk{l}"))
                turn(f"mk{l}", [(48 * c, mk[0:48, P * c:P * c + P]) for c in range(TC)]).then_inc(*jobs.fills(f"mk{l}"))
                eng.wait_ge(*jobs.is_drained(f"mk{l}"))
                job = f"ps{l}"
                if jobs.new(job) > 1:
                    eng.wait_ge(*jobs.is_free(job))
                o = jobs.bank(job)
                project([(o[:, 0:48], [(tri_le, mt[:, 0, :])]),
                                 (o[:, 48:96], [(ones, mt[:, 0, :]), (tri_le, mt[:, 1, :])])]).then_inc(*jobs.fills(job))
                for s in streams:
                    eng.wait_ge(flag("selection"), sum(len(q) for q in ([0, 1], [0])[:l]) + s + 1)
                    for k in range(KD):
                        job = f"ga{l}{s}{k}"
                        if jobs.new(job) > 1:
                            eng.wait_ge(*jobs.is_free(job))
                        o = jobs.bank(job)
                        project([(o[:, :], [(tokens_of[:, 2 * s + c, P * k:P * k + P], sel_of[2 * s][:, c, :])
                                                    for c in range(TC)])]).then_inc(*jobs.fills(job))
                for s in streams:
                    eng.wait_ge(flag("weighted"), sum(len(q) for q in ([0, 1], [0])[:l]) + s + 1)
                    for g in range(0, 4, 2):
                        if jobs.new(f"GT{l}{s}{g}") > 1:
                            eng.wait_ge(*jobs.is_free(f"GT{l}{s}{g}"))
                        turn(f"GT{l}{s}{g}", [(N * j + P * c, sel_of[2 * s + 1][:, c, P * (g + j):P * (g + j) + P])
                                              for j in range(2) for c in range(TC)]).then_inc(*jobs.fills(f"GT{l}{s}{g}"))

            def experts(l, G):
                M = P // G
                W = FF // G
                first = first_experts[l]
                at = [(first + j) % SLOTS for j in range(6)]
                base = [landed[f"x{l}_{j}"] for j in range(6)]
                with eng.Fori(0, 4) as g4:
                    for i in range(4):
                        e = g4 * 4 + i

                        def stage_in(which):
                            for half in range(2):
                                j = 2 * which + half
                                eng.wait_ge(arrived[at[j]], g4 * 64 + (16 * i + base[j]))
                                yield half, ring[:, at[j], :].rearrange("p (k n) -> p k n", n=FF)

                        eng.wait_ge(flag("expert_tokens"), g4 * 4 + (E * l + i + 1))
                        xc = x_cur[:, i % 2, 0:KD * M].rearrange("p (k m) -> p k m", m=M)
                        for which in range(2):
                            for half, w in stage_in(which):
                                for k in range(4):
                                    for q in range(G):
                                        ins = mm(banks[M * q:M * q + M, which, 0:W], xc[:, 4 * half + k, :],
                                                 w[:, k, W * q:W * q + W], start=(half == 0 and k == 0),
                                                 stop=(half == 1 and k == 3), skip_group_check=True)
                                ins.then_inc(flag("experts_pe"), 1)
                        eng.wait_ge(flag("expert_gated"), g4 * 4 + (E * l + i + 1))
                        for j in range(W // P):
                            ins = nc.tensor.transpose(banks[:, 2, P * j:P * j + P], x_g[:, P * j:P * j + P], ident)
                        ins.then_inc(flag("experts_pe"), 1)
                        eng.wait_ge(flag("expert_gatedT"), g4 * 4 + (E * l + i + 1))
                        gT = x_gT[:, 0:W].rearrange("p (j q m) -> p j q m", q=G, m=M)
                        for half, w in stage_in(2):
                            for k in range(4):
                                kk = 4 * half + k
                                for q in range(G):
                                    ins = mm(banks[M * q:M * q + M, 3, 0:W], gT[:, kk % (W // P), kk // (W // P), :],
                                             w[:, k, W * q:W * q + W], start=(kk == 0), stop=(kk == 7),
                                             skip_group_check=True)
                            ins.then_inc(flag("experts_pe"), 1)

            def combine(l, streams):
                eng.wait_ge(flag("y_by_act"), E * (l + 1))
                eng.wait_ge(flag("y_by_dve"), E * (l + 1))
                for s in streams:
                    for n in range(4):
                        job = f"cb{l}{s}{n}"
                        if jobs.new(job) > 1:
                            eng.wait_ge(*jobs.is_free(job))
                        o = jobs.bank(job)
                        project([(o[:, N * j:N * j + N],
                                          [(y_of[s][:, g, P * (2 * n + j):P * (2 * n + j) + P], GT[s][:, g, :])
                                           for g in range(4)]) for j in range(2)]).then_inc(*jobs.fills(job))

            routed(0, (0, 1), "h4")
            eng.wait_ge(*jobs.is_drained("ga017"))
            eng.wait_ge(*jobs.is_drained("ga016"))
            for s in range(2):
                for g in range(0, 4, 2):
                    eng.wait_ge(*jobs.is_drained(f"GT0{s}{g}"))
            experts(0, 2)
            combine(0, (1, 0))

            sum_squares("o1", 1)
            sum_squares("o1", 0)
            eng.wait_ge(flag("h5_0"), 1)
            eng.wait_ge(flag("h5_0_v"), 1)
            eng.wait_ge(flag("h5_1"), 1)
            eng.wait_ge(flag("h5_1_v"), 1)
            eng.wait_ge(*arrives("ock"))
            w = slot("ock", 288)
            for j in range(2):
                if jobs.new(f"ock{j}") > 1:
                    eng.wait_ge(*jobs.is_free(f"ock{j}"))
                o = jobs.bank(f"ock{j}")
                project([(o[:, :], [(w[:, k, P * j:P * j + P], hT[:, :, k, :]) for k in range(KD)])]).then_inc(*jobs.fills(f"ock{j}"))
            if jobs.new("okr") > 1:
                eng.wait_ge(*jobs.is_free("okr"))
            o = jobs.bank("okr")
            project([(o[64:96, :], [(w[:, k, 256:288], hT[:, :, k, :]) for k in range(KD)])]).then_inc(*jobs.fills("okr"))
            used("ock", "okr")
            eng.wait_ge(*arrives("ocq"))
            w = slot("ocq", 384)
            for j in range(3):
                if jobs.new(f"ocq{j}") > 1:
                    eng.wait_ge(*jobs.is_free(f"ocq{j}"))
                o = jobs.bank(f"ocq{j}")
                project([(o[:, 0:N], [(w[:, k, P * j:P * j + P], hlat[:, k, :]) for k in range(KD)])]).then_inc(*jobs.fills(f"ocq{j}"))
            used("ocq", "ocq2")
            for a in range(2):
                conv_inputs("ogb", a)
            eng.wait_ge(flag("odd_consts_in"), 16)
            eng.wait_ge(*jobs.is_drained("okr"))
            if jobs.new("osk") > 1:
                eng.wait_ge(*jobs.is_free("osk"))
            o = jobs.bank("osk")
            mm(o[64:96, 0:N], phase[64:96, M_SWAP + 64:M_SWAP + 96], o_kr[64:96, 0:N], start=True, stop=True).then_inc(*jobs.fills("osk"))
            eng.wait_ge(flag("sq_kv"), 1)
            if jobs.new("ss_kv") > 1:
                eng.wait_ge(*jobs.is_free("ss_kv"))
            o = jobs.bank("ss_kv")
            project([(o[:, :], [(ones, o_sq[:, j, :]) for j in range(2)])]).then_inc(*jobs.fills("ss_kv"))
            eng.wait_ge(flag("sq_q"), 1)
            if jobs.new("ss_q") > 1:
                eng.wait_ge(*jobs.is_free("ss_q"))
            o = jobs.bank("ss_q")
            sq3 = o_sq.rearrange("p a n -> p (a n)")[:, 0:768].rearrange("p (a n) -> p a n", n=N)
            project([(o[:, 0:N], [(ones, sq3[:, j, :]) for j in range(3)])]).then_inc(*jobs.fills("ss_q"))
            eng.wait_ge(*arrives("ukv"))
            w = slot("ukv", D)
            eng.wait_ge(flag("kv_normed"), 1)
            for a in range(4):
                job = f"ok{a}"
                if jobs.new(job) > 1:
                    eng.wait_ge(*jobs.is_free(job))
                o = jobs.bank(job)
                for j in range(2):
                    for z in range(2):
                        h = 2 * a + z
                        ins = mm(o[64 * z:64 * z + 64, :], w[:, j, P * h:P * h + 64], o_ckv[:, j, :],
                                 start=(j == 0), stop=(j == 1), skip_group_check=True)
                ins.then_inc(*jobs.fills(job))
            wv = w.rearrange("p k (h z d) -> p k h z d", z=2, d=64)
            for c in range(4):
                job = f"ov{c}"
                if jobs.new(job) > 1:
                    eng.wait_ge(*jobs.is_free(job))
                o = jobs.bank(job)
                project([(o[:, :], [(o_ckv[:, j, P * c:P * c + P], wv[:, j, :, 1, :]) for j in range(2)])]).then_inc(*jobs.fills(job))
            used("ukv", job)
            eng.wait_ge(*arrives("uq"))
            w = slot("uq", 768)
            eng.wait_ge(flag("q_normed"), 1)
            for a in range(4):
                job = f"oq{a}"
                if jobs.new(job) > 1:
                    eng.wait_ge(*jobs.is_free(job))
                o = jobs.bank(job)
                project([(o[0:96, N * j:N * j + N],
                                  [(w[:, k, 96 * (2 * a + j):96 * (2 * a + j) + 96], o_cq[:, k, :])
                                   for k in range(3)]) for j in range(2)]).then_inc(*jobs.fills(job))
            used("uq", job)
            for a in range(4):
                eng.wait_ge(*jobs.is_drained(f"oq{a}"))
                if jobs.new(f"osq{a}") > 1:
                    eng.wait_ge(*jobs.is_free(f"osq{a}"))
                o = jobs.bank(f"osq{a}")
                mm(o[0:96, :], phase[0:96, M_SWAP:M_SWAP + 96], o_q[0:96, 2 * a:2 * a + 2, :],
                        start=True, stop=True).then_inc(*jobs.fills(f"osq{a}"))
            for a in range(2):
                conv_inputs("ogc", a)
            eng.wait_ge(flag("rope_odd"), 4)
            eng.wait_ge(flag("kr_copied"), 1)
            eng.wait_ge(flag("kr_copied_by_pool"), 1)
            for a in range(4):
                eng.wait_ge(*jobs.is_drained(f"ok{a}"))
            for c in range(4):
                eng.wait_ge(*jobs.is_drained(f"ov{c}"))
            att_p, att_pT = o_p, o_pT
            attention("oa", ODD_TILES, lambda s, c, h: (o_q[0:96, h, P * c:P * c + P], o_k[0:96, h, :]),
                      lambda s, q, h: o_v[:, q, 64 * h:64 * h + 64])
            eng.wait_ge(flag("att_out_odd"), 1)
            for c in range(TC):
                if jobs.new(f"oct{c}") > 1:
                    eng.wait_ge(*jobs.is_free(f"oct{c}"))
                turn(f"oct{c}", [(P * j, o_o[:, c, P * j:P * j + P]) for j in range(4)]).then_inc(*jobs.fills(f"oct{c}"))
            for c in range(TC):
                eng.wait_ge(*jobs.is_drained(f"oct{c}"))
            eng.wait_ge(flag("conv"), 1)
            for b in range(2):
                eng.wait_ge(*arrives(f"oo{b}"))
                w = slot(f"oo{b}", 512)
                for a in range(2):
                    job = f"oo{2 * b + a}"
                    if jobs.new(job) > 1:
                        eng.wait_ge(*jobs.is_free(job))
                    o = jobs.bank(job)
                    project([(o[:, N * j:N * j + N],
                                      [(w[:, k, P * (2 * a + j):P * (2 * a + j) + P], o_cat[:, k, :])
                                       for k in range(KD)]) for j in range(2)]).then_inc(*jobs.fills(job))
                used(f"oo{b}", job)
            routed(1, (0,), "h6")
            eng.wait_ge(*jobs.is_drained("ga107"))
            eng.wait_ge(*jobs.is_drained("ga106"))
            for g in range(0, 4, 2):
                eng.wait_ge(*jobs.is_drained(f"GT10{g}"))
            experts(1, 4)
            combine(1, (0,))
            sum_squares("out", 0)
            for a in range(2):
                eng.wait_ge(flag("out_normed"), 4 * a + 4)
                for c in range(TC):
                    if jobs.new(f"out{c}{a}") > 1:
                        eng.wait_ge(*jobs.is_free(f"out{c}{a}"))
                    turn(f"out{c}{a}", [(P * j, xT[:, 4 * a + j, P * c:P * c + P]) for j in range(4)]).then_inc(*jobs.fills(f"out{c}{a}"))

        @block.sync
        def _(eng):
            def load(i):
                name, parts = blocks[i]
                for off, (a, w), src in parts:
                    dst = ring[:, i % SLOTS, 0:a * w].rearrange("p (a w) -> p a w", w=w)
                    eng.dma_start(dst[:, :, off:off + src.shape[2]], src).then_inc(arrived[i % SLOTS], 16)

            def release(i):
                if i >= SLOTS:
                    eng.wait_ge(*jobs.is_filled(last_job[blocks[i - SLOTS][0]]))

            eng.dma_start(const[:], t["const_all"]).then_inc(flag("consts_in"), 16)
            for tile_, row, src in vector_loads:
                eng.dma_start(vrows[row:row + src.shape[0], tile_, :], src).then_inc(flag("vectors_in"), 16)
            eng.dma_start(stage[0], t["x"][0].rearrange("(c p) d -> p c d", p=P)).then_inc(flag("tokens_in"), 16)
            eng.dma_start(stage[1], t["ctx"][0].rearrange("(c p) d -> p c d", p=P)).then_inc(flag("tokens_in"), 16)
            for i in range(4):
                load(i)
            eng.dma_start(phase[:], t["const_ret"]).then_inc(flag("ret_consts_in"), 16)
            eng.dma_start(mg_raw, rows_of(w_in, 4096, 16)).then_inc(flag("gate_weights_in"), 16)
            eng.wait_ge(flag("small_set"), 1)
            eng.dma_start(lg, t["ret_decay_logit"].rearrange("a d h -> a (d h)").broadcast_to((P, 8)))\
               .then_inc(flag("decay_in"), 16)
            for y in range(4):
                r = 64 * (y % 2) + 32 * (y // 2)
                eng.dma_start(gate_bias[r:r + 4, :],
                              t["mlstm_gate_bias"][0, y:y + 1, :].rearrange("a h -> h a"))\
                   .then_inc(flag("gate_bias_in"), 16)
            eng.dma_start(sink, t["ev_sink_2"].broadcast_to((P, AH))).then_inc(flag("sink_in"), 16)
            for i in range(4, index["m_up"] + SLOTS):
                release(i)
                load(i)
            release(index["m_up"] + SLOTS)
            eng.dma_start(stage2, t["ctx_2"][0].rearrange("(c p) d -> p c d", p=P)).then_inc(flag("tokens_in"), 16)
            eng.dma_start(phase[:, 0:M_END], t["const_even"]).then_inc(flag("even_consts_in"), 16)
            eng.dma_start(e_gain, t["ev_sgu_norm_g_2"].broadcast_to((P, 512))).then_inc(flag("gain_in"), 16)
            eng.dma_start(ws_raw, t["ev_sgu_w_2"][0].rearrange("g p q -> p g q")).then_inc(flag("ws_in"), 16)
            for l in range(DEPTH2):
                eng.dma_start(rws[l], t["router_w_2"][l].rearrange("(k p) e -> p k e", p=P)).then_inc(flag("router_in"), 16)
            load(index["m_up"] + SLOTS)
            for i in range(index["m_up"] + SLOTS + 1, first_experts[0]):
                release(i)
                load(i)

            def experts(l):
                first = first_experts[l]
                parts = [(w, half) for w in ("exp_w1_2", "exp_w3_2", "exp_w2_2") for half in range(2)]

                def part(e, j):
                    w, half = parts[j]
                    src = t[w][l][bass.ds(e, 1)] if not isinstance(e, int) else t[w][l][e:e + 1]
                    src = src.rearrange("a (k p) n -> p (a k) n", p=P)[:, 4 * half:4 * half + 4, :]
                    s = (first + j) % SLOTS
                    eng.dma_start(ring[:, s, :].rearrange("p (k n) -> p k n", n=FF), src).then_inc(arrived[s], 16)

                for j in range(6):
                    release(first + j)
                    part(0, j)
                done = (1, 2, 3, 4, 6, 7)
                with eng.Fori(1, E) as e:
                    for j in range(6):
                        eng.wait_ge(flag("experts_pe"), e * XJ + (XJ * E * l - XJ + done[j]))
                        part(e, j)
                return done

            def after_experts(l, lo, hi, done):
                for i in range(lo, hi):
                    j = i - first_experts[l] - 6 * E
                    if j < SLOTS:
                        eng.wait_ge(flag("experts_pe"), XJ * E * (l + 1) - XJ + done[j])
                    else:
                        release(i)
                    load(i)

            done = experts(0)
            eng.wait_ge(flag("att_out_even"), 1)
            eng.dma_start(phase[:, 0:M_END], t["const_odd"]).then_inc(flag("odd_consts_in"), 16)
            after_experts(0, index["ock"], first_experts[1], done)
            experts(1)
            for a in range(2):
                for c in range(TC):
                    eng.wait_ge(*jobs.is_drained(f"out{c}{a}"))
                eng.dma_start(out.rearrange("a (c p) d -> p (a c) d", p=P)[:, :, 512 * a:512 * a + 512],
                              stage[0][:, :, 512 * a:512 * a + 512]).then_inc(flag("out_written"), 16)
            eng.wait_ge(flag("out_written"), 32)

        def flat(a):
            names = "abcd"[:len(a.shape) - 1]
            return a.rearrange(f"p {' '.join(names)} -> p ({' '.join(names)})") if len(names) > 1 else a

        def columns(a, n):
            return a.unsqueeze(2).broadcast_to((a.shape[0], a.shape[1], n))

        def over(a, n):
            return a.unsqueeze(1).broadcast_to((a.shape[0], n, a.shape[1]))

        def shift_of(L, which, c, k):
            return mod[:, L, KD * which + k, c:c + 1]

        x_junk = carve(15648, P)

        def x_slots(l):
            return carve(0, E, KD, CAP * (2 - l))

        @block.scalar
        def _(eng):
            act = Lane(jobs, flag("act_done"), flag)
            A = nc.scalar.activation

            def mod_copy(l, b):
                eng.wait_ge(*jobs.is_filled(f"mod_{l}{b}"))
                o = jobs.bank(f"mod_{l}{b}")
                A(modrow[:], o[:, :], ACT.Copy).then_inc(*act.frees(f"mod_{l}{b}"))

            def squares(s, src, residuals=None, chunks=None):
                eng.wait_ge(*act.last)
                for a in range(4):
                    for job in (residuals[a] if residuals else ()):
                        eng.wait_ge(*jobs.is_drained(job))
                    if chunks:
                        eng.wait_ge(flag(chunks), 2 * a + 2)
                    A(hT[:, s, 2 * a:2 * a + 2], src[:, 2 * a:2 * a + 2], ACT.Square).then_inc(*act.raises("squares"))

            def stds(tag, s, width=N, n=D):
                eng.wait_ge(*jobs.is_filled(f"{tag}_ss{s}"))
                o = jobs.bank(f"{tag}_ss{s}")
                eng.wait_ge(*act.last)
                A(o[:, 0:width], o[:, 0:width], ACT.Sqrt, scale=1.0 / n, bias=eps).then_inc(*act.raises("std"))

            def affine(tag, s, L, c, which, hname):
                eng.wait_ge(*jobs.is_drained(f"{tag}_ss{s}"))
                for k in range(KD // 2):
                    ins = A(hT[:, s, k, :], hT[:, s, k, :], ACT.Identity, scale=gainA[:, s, k:k + 1],
                            bias=shift_of(L, which, c, k))
                ins.then_inc(*act.raises(hname))

            eng.wait_ge(flag("small_set"), 1)
            eng.wait_ge(*jobs.is_drained(f"vec{V_TILES - 1}"))
            for i, v in enumerate((V_C, V_CC, V_C2, V_CC2)):
                ins = A(sil_c[:, :, i], vec[:, v:v + KD], ACT.Silu)
            ins.then_inc(*act.raises("silu_c"))
            for a in range(4):
                eng.wait_ge(*jobs.is_filled(f"xt0{a}"))
                o = jobs.bank(f"xt0{a}")
                A(xT[:, 2 * a:2 * a + 2, :], o[:, :].rearrange("p (b n) -> p b n", b=2), ACT.Copy).then_inc(*act.frees(f"xt0{a}"))
            for a in range(4):
                eng.wait_ge(*jobs.is_drained(f"xt1{a}"))
            squares(1, cT)
            squares(0, xT)
            stds("n1", 1)
            stds("n1", 0)
            for b in range(4):
                mod_copy("a", b)
            eng.wait_ge(flag("first_gains"), 1)
            affine("n1", 1, 0, 1, 0, "h1_1")
            affine("n1", 0, 0, 0, 0, "h1_0")

            def log_sigmoid_part(dst, x, flagged):
                eng.wait_ge(*act.last)
                A(dst, x, ACT.Abs).then_inc(*act.steps())
                eng.wait_ge(*act.last)
                A(dst, dst, ACT.Exp, scale=-1.0).then_inc(*act.steps())
                eng.wait_ge(*act.last)
                A(dst, dst, ACT.Ln, bias=ones[0:dst.shape[0], 0:1]).then_inc(*act.raises(flagged))

            eng.wait_ge(flag("decay_in"), 16)
            log_sigmoid_part(segs[:, 0:8], lg, "log1p")
            eng.wait_ge(flag("source_distance"), 1)
            eng.wait_ge(*act.last)
            A(small[:, 104:120], small[:, 104:120], ACT.Exp).then_inc(*act.raises("source_decay"))
            for i, s in enumerate((1, 0)):
                eng.wait_ge(flag("forget_rows"), i + 1)
                log_sigmoid_part(rL[0:64, :], rF[0:64, :], "log1p")
                eng.wait_ge(flag("stabilised"), i + 1)
                eng.wait_ge(*act.last)
                if s == 1:
                    A(rC[0:64, :], rG[0:64, :], ACT.Exp, bias=neg_mc[0:64, :]).then_inc(*act.raises("row_exp"))
                else:
                    A(rG[0:64, :], rG[0:64, :], ACT.Exp, scale=-1.0).then_inc(*act.raises("row_exp"))
            for n, dst in (("rk", rkT), ("rv", rv), ("mk", mkT), ("mv", mv)):
                for c in range(TC):
                    if n == "rv":
                        eng.wait_ge(*jobs.is_filled(f"c_rv{c}"))
                        o = jobs.bank(f"c_rv{c}")
                        A(vc_r[:, c, :], o[:, :], ACT.Copy).then_inc(*act.frees(f"c_rv{c}"))
                    if n == "mv":
                        eng.wait_ge(*jobs.is_filled(f"c_mv{c}"))
                        o = jobs.bank(f"c_mv{c}")
                        A(vc_m[:, c, :, 0:P], o[:, :].rearrange("p (h d) -> p h d", h=HEADS), ACT.Copy).then_inc(*act.frees(f"c_mv{c}"))
                for c in range(TC):
                    job = f"x_{n}{c}"
                    eng.wait_ge(*jobs.is_filled(job))
                    o = jobs.bank(job)
                    if n[1] == "k":
                        A(flat(dst[:, 2 * c:2 * c + 2, :]), o[:, :], ACT.Copy, scale=HD_SCALE).then_inc(*act.frees(job))
                    elif n == "rv":
                        A(rv[:, c, :], o[:, :], ACT.Copy).then_inc(*act.frees(job))
                    else:
                        A(mv[:, c, :, 0:P], o[:, :].rearrange("p (h d) -> p h d", h=HEADS), ACT.Copy).then_inc(*act.frees(job))
            eng.wait_ge(*jobs.is_filled("s_ml11"))
            eng.wait_ge(*act.last)
            for h in range(HEADS):
                A(decay[:, h, 0:N], phase[:, R_TS:R_TS + N], ACT.Exp, scale=lg[:, h:h + 1]).then_inc(*act.steps())
                ins = A(decay[:, h, N:2 * N], phase[:, R_ST:R_ST + N], ACT.Exp, scale=lg[:, 4 + h:5 + h])
                if h < HEADS - 1:
                    ins.then_inc(*act.steps())
            ins.then_inc(*act.raises("decays"))
            for n, dst in (("rq", rqT), ("mq", mqT)):
                for c in range(TC):
                    eng.wait_ge(*jobs.is_filled(f"x_{n}{c}"))
                    o = jobs.bank(f"x_{n}{c}")
                    A(flat(dst[:, 2 * c:2 * c + 2, :]), o[:, :], ACT.Copy).then_inc(*act.frees(f"x_{n}{c}"))
            for c in range(TC):
                eng.wait_ge(*jobs.is_filled(f"x_rg{c}"))
                o = jobs.bank(f"x_rg{c}")
                A(rg[:, c, :], o[:, :], ACT.Silu).then_inc(*act.frees(f"x_rg{c}"))
            for c in range(TC):
                eng.wait_ge(*jobs.is_filled(f"x_mo{c}"))
                o = jobs.bank(f"x_mo{c}")
                A(mo[:, c, :], o[:, :], ACT.Sigmoid).then_inc(*act.frees(f"x_mo{c}"))
            for h in range(HEADS):
                if h >= 2:
                    eng.wait_ge(*jobs.is_filled(f"ro{h - 2}"))
                for d in range(2):
                    eng.wait_ge(*act.last)
                    A(q_ret[:, h % 2, d, :], phase[:, (R_T1, R_TR)[d]:(R_T1, R_TR)[d] + N], ACT.Exp,
                               scale=lg[:, 4 * d + h:4 * d + h + 1]).then_inc(*act.raises("ret_decay"))
                mod_copy("a", 4 + h)
            eng.wait_ge(flag("mc_rep"), 1)
            eng.wait_ge(*jobs.is_filled("ro3"))
            eng.wait_ge(flag("ret_q"), 8)

            def ml_exps(h):
                if h >= 2:
                    eng.wait_ge(*jobs.is_filled(f"mo{h - 2}1"))
                for d in range(2):
                    job = f"cr{h}{d}"
                    eng.wait_ge(*jobs.is_filled(job))
                    o = jobs.bank(job)
                    eng.wait_ge(flag("ml_w"), 2 * h + d + 1)
                    A(q_ml[:, h % 2, d, :], o[:, 0:N], ACT.Exp, scale=-1.0,
                                bias=mc_rep[:, 32 * d + h:32 * d + h + 1]).then_inc(*act.frees(job))
                    A(p_ml[:, h % 2, d, :], p_ml[:, h % 2, d, :], ACT.Exp, scale=-1.0).then_inc(*act.raises("ml_weighted"))

            def ml_abs(h):
                for c in range(TC):
                    eng.wait_ge(*jobs.is_filled(f"mo{h}{c}"))
                    o = jobs.bank(f"mo{h}{c}")
                    eng.wait_ge(*act.last)
                    A(dn[:, (2 * h + c) % 4, :], o[:, 0:258].rearrange("p (d n) -> p d n", d=2)[:, :, P],
                               ACT.Abs).then_inc(*act.raises("abs_den"))

            ml_exps(0)
            for h in range(HEADS):
                mod_copy("a", 8 + h)
                ml_abs(h)
                if h + 1 < HEADS:
                    ml_exps(h + 1)
            for m, y in enumerate((ret, ml)):
                if m == 0:
                    eng.wait_ge(*jobs.is_drained("ro3"))
                else:
                    eng.wait_ge(flag("ml_gated"), 1)
                for c in range(TC):
                    for h in range(HEADS):
                        i = 8 * m + 4 * c + h
                        eng.wait_ge(*act.last)
                        A(x_junk, y[:, c, P * h:P * h + P], ACT.Square, accum_out=segs[:, i:i + 1]).then_inc(*act.steps())
                eng.wait_ge(*act.last)
                A(segs[:, 8 * m:8 * m + 8], segs[:, 8 * m:8 * m + 8], ACT.Sqrt, scale=1.0 / P, bias=eps).then_inc(*act.raises("head_std"))
            eng.wait_ge(flag("y_normed"), 2)
            for b in range(4):
                for a in range(2):
                    eng.wait_ge(*jobs.is_filled(f"bg{b}{a}"))
                    o = jobs.bank(f"bg{b}{a}")
                    dst = (sig_r, sig_m)[b // 2][:, 4 * (b % 2) + 2 * a:4 * (b % 2) + 2 * a + 2, :]
                    A(flat(dst), o[:, :], ACT.Sigmoid).then_inc(*act.frees(f"bg{b}{a}"))
            for a in range(2):
                eng.wait_ge(*jobs.is_filled(f"yT0{a}"))
                o = jobs.bank(f"yT0{a}")
                A(flat(yT[:, 2 * a:2 * a + 2, :]), o[:, :], ACT.Copy).then_inc(*act.frees(f"yT0{a}"))
            squares(0, xT, [[f"wo{a}"] for a in range(4)])
            stds("n2", 0)
            affine("n2", 0, 0, 0, 3, "h2_0")
            for b in range(KF // 2):
                for a in range(2):
                    j = 2 * b + a
                    eng.wait_ge(*jobs.is_filled(f"fi{j}"))
                    o = jobs.bank(f"fi{j}")
                    if j >= 2:
                        eng.wait_ge(*jobs.is_drained(f"fi{j - 2}"))
                    A(f_sil[:, j % 2, :], o[:, 0:N], ACT.Silu).then_inc(*act.raises("ffn_silu"))
                mod_copy("b", b)
            mod_copy("b", 11)
            for a in range(4):
                eng.wait_ge(*jobs.is_filled(f"yt{a}"))
                o = jobs.bank(f"yt{a}")
                A(cT[:, 2 * a:2 * a + 2, :], o[:, :].rearrange("p (b n) -> p b n", b=2), ACT.Copy).then_inc(*act.frees(f"yt{a}"))
            squares(1, cT)
            stds("e1", 1)
            affine("e1", 1, 1, 1, 0, "h3_1")
            squares(0, xT, [[f"fo{2 * a}", f"fo{2 * a + 1}"] for a in range(4)])
            stds("nf", 0)

            def attention(tag, tiles, p, pT, scale, with_sink):
                T = len(tiles)
                for i in range(T + 3):
                    if 2 <= i < T + 2:
                        j = i - 2
                        eng.wait_ge(*jobs.is_filled(f"{tag}_t{j}"))
                        o = jobs.bank(f"{tag}_t{j}")
                        kc = 4 if tiles[j][0] == 0 else 2
                        if j >= 2:
                            eng.wait_ge(*jobs.is_filled(f"{tag}_o{j - 2}"))
                        A(pT[:, j % 2, 0:kc, :], o[:, 0:P * kc].rearrange("p (k n) -> p k n", n=P), ACT.Copy).then_inc(*act.frees(f"{tag}_t{j}"))
                    if i < T:
                        s, c, h = tiles[i]
                        w = 512 if s == 0 else N
                        eng.wait_ge(*jobs.is_filled(f"{tag}_s{i}"))
                        o = jobs.bank(f"{tag}_s{i}")
                        if i >= 2:
                            eng.wait_ge(*jobs.is_filled(f"{tag}_t{i - 2}"))
                        eng.wait_ge(flag(f"neg_max_{tag}"), i + 1)
                        if with_sink:
                            A(att[:, i % 8, 3:4], sink[:, h:h + 1], ACT.Exp, bias=att[:, i % 8, 1:2]).then_inc(*act.steps())
                        A(p[:, i % 2, 0:w], o[:, 0:w], ACT.Exp, bias=att[:, i % 8, 1:2], scale=scale,
                                    accum_out=att[:, i % 8, 2:3]).then_inc(*act.frees(f"{tag}_s{i}"))
                    if tag == "ea" and i == 24:
                        eng.wait_ge(flag("sgu_var"), 1)
                        eng.wait_ge(*act.last)
                        A(lnst[:, :, 2], lnst[:, :, 2], ACT.Sqrt, scale=1.0 / 512, bias=eps).then_inc(*act.raises("sgu_std"))
                    if tag == "ea" and i % 3 == 1:
                        mod_copy("c", i // 3)
                    if tag == "oa" and i in CONV_AT:
                        n, a = CONV_AT[i]
                        eng.wait_ge(*jobs.is_filled(f"{n}{a}"))
                        o = jobs.bank(f"{n}{a}")
                        A(flat(o_hh[:, 2 * a:2 * a + 2, :]), o[:, :], ACT.Copy).then_inc(*act.frees(f"{n}{a}"))

            squares(0, xT, chunks="x1_ready")
            stds("e1", 0)
            affine("e1", 0, 1, 0, 0, "h3_0")
            eng.wait_ge(*jobs.is_filled("e_k"))
            o = jobs.bank("e_k")
            A(e_k, o[:, :], ACT.Copy).then_inc(*act.frees("e_k"))
            for j in range(4):
                eng.wait_ge(*jobs.is_filled(f"e_q{j}"))
                o = jobs.bank(f"e_q{j}")
                A(e_q[:, j, :], o[:, :], ACT.Copy).then_inc(*act.frees(f"e_q{j}"))
            for c in range(4):
                eng.wait_ge(*jobs.is_filled(f"eu{c}"))
                o = jobs.bank(f"eu{c}")
                A(e_u[:, c, :], o[:, :], ACT.Gelu_apprx_tanh).then_inc(*act.frees(f"eu{c}"))
            for c in range(4):
                eng.wait_ge(*jobs.is_filled(f"ew{c}"))
                o = jobs.bank(f"ew{c}")
                A(e_w[:, c, :], o[:, :], ACT.Gelu_apprx_tanh, accum_out=lnst[:, c, 0:1]).then_inc(*act.frees(f"ew{c}"))
            eng.wait_ge(flag("sink_in"), 16)
            attention("ea", EVEN_TILES, e_p, e_pT, 64.0 ** -0.5, True)
            for c in range(4):
                eng.wait_ge(*jobs.is_filled(f"ect{c}0"))
                o = jobs.bank(f"ect{c}0")
                A(e_cat[:, 0:4, P * c:P * c + P], o[:, :].rearrange("p (j n) -> p j n", n=P), ACT.Copy).then_inc(*act.frees(f"ect{c}0"))

            def routed(l, streams, tag, L, hname, residuals):
                for s in streams:
                    squares(s, (xT, cT)[s], residuals)
                for s in streams:
                    stds(tag, s)
                for s in streams:
                    affine(tag, s, L, s, 3, f"{hname}_{s}")
                eng.wait_ge(flag("logits"), l + 1)
                eng.wait_ge(*act.last)
                A(logit[:, 0:32 * len(streams)], logit[:, 0:32 * len(streams)], ACT.Exp).then_inc(*act.raises("router_exp"))
                for s in streams:
                    for c in range(TC):
                        eng.wait_ge(*jobs.is_filled(f"th{l}{s}{c}1"))
                        o = jobs.bank(f"th{l}{s}{c}1")
                        A(tokens_of[:, 2 * s + c, 512:1024], o[:, :], ACT.Copy).then_inc(*act.frees(f"th{l}{s}{c}1"))
                for s in streams:
                    for k in range(1, KD, 2):
                        eng.wait_ge(*jobs.is_filled(f"ga{l}{s}{k}"))
                        o = jobs.bank(f"ga{l}{s}{k}")
                        A(x_slots(l)[:, :, k, CAP * s:CAP * s + CAP], o[:, :].rearrange("p (e m) -> p e m", e=E), ACT.Copy).then_inc(*act.frees(f"ga{l}{s}{k}"))

            def experts(l, G):
                W = FF // G
                eng.wait_ge(flag("expert_tokens"), E * l + 1)
                with eng.Fori(0, 4) as g4:
                    for i in range(4):
                        n = g4 * (4 * XJ) + (XJ * (E * l + i))
                        eng.wait_ge(flag("experts_pe"), n + 2)
                        A(x_sil[:, 0:W], banks[:, 0, 0:W], ACT.Silu).then_inc(flag("expert_silu"), 1)
                        eng.wait_ge(flag("experts_pe"), n + 5)
                        A(x_gT[:, 0:W], banks[:, 2, 0:W], ACT.Copy).then_inc(flag("expert_gatedT"), 1)
                        eng.wait_ge(flag("experts_pe"), n + 7)
                        for q in range(G // 2):
                            src = banks[P // G * q:P // G * q + CAP, 3, 0:W]
                            ins = A(y_of[0][CAP * i:CAP * i + CAP, bass.ds(g4, 1), W * q:W * q + W],
                                    src.unsqueeze(1), ACT.Copy)
                            if G == 2:
                                src = banks[32:64, 3, 0:W]
                                ins = A(y_of[1][CAP * i:CAP * i + CAP, bass.ds(g4, 1), 0:W], src.unsqueeze(1), ACT.Copy)
                        ins.then_inc(flag("y_by_act"), 1)
                act.last = (flag("y_by_act"), E * (l + 1))

            routed(0, (0, 1), "r0", 1, "h4", [[f"eo{2 * a}", f"eo{2 * a + 1}"] for a in range(4)])
            experts(0, 2)
            eng.wait_ge(*jobs.is_drained("cb012"))
            eng.wait_ge(*jobs.is_drained("cb013"))
            squares(1, cT, [[f"cb01{n}"] for n in range(4)])
            squares(0, xT, [[f"cb00{n}"] for n in range(4)])
            for s in (1, 0):
                stds("o1", s)
            for s in (1, 0):
                affine("o1", s, 2, s, 0, f"h5_{s}")
            for j in range(2):
                eng.wait_ge(*jobs.is_filled(f"ock{j}"))
                o = jobs.bank(f"ock{j}")
                A(o_ckv[:, j, :], o[:, :], ACT.Copy).then_inc(*act.frees(f"ock{j}"))
            eng.wait_ge(*jobs.is_filled("okr"))
            o = jobs.bank("okr")
            A(o_kr[64:96, :], o[64:96, :], ACT.Copy).then_inc(*act.frees("okr"))
            eng.wait_ge(*act.last)
            A(o_sq[:], o_ckv[:], ACT.Square).then_inc(*act.raises("sq_kv"))
            for j in range(3):
                eng.wait_ge(*jobs.is_filled(f"ocq{j}"))
                o = jobs.bank(f"ocq{j}")
                A(o_cq[:, j, :], o[:, 0:N], ACT.Copy).then_inc(*act.frees(f"ocq{j}"))
            for a in range(2):
                eng.wait_ge(*jobs.is_filled(f"ogb{a}"))
                o = jobs.bank(f"ogb{a}")
                A(flat(o_gb[:, 2 * a:2 * a + 2, :]), o[:, :], ACT.Copy).then_inc(*act.frees(f"ogb{a}"))
            eng.wait_ge(*jobs.is_filled("ss_kv"))
            o = jobs.bank("ss_kv")
            eng.wait_ge(*act.last)
            A(o[:, :], o[:, :], ACT.Sqrt, scale=1.0 / 256, bias=eps).then_inc(*act.raises("std"))
            eng.wait_ge(*act.last)
            A(flat(o_sq)[:, 0:768], flat(o_cq), ACT.Square).then_inc(*act.raises("sq_q"))
            eng.wait_ge(*jobs.is_filled("ss_q"))
            o = jobs.bank("ss_q")
            eng.wait_ge(*act.last)
            A(o[:, 0:N], o[:, 0:N], ACT.Sqrt, scale=1.0 / 384, bias=eps).then_inc(*act.raises("std"))
            for a in range(4):
                eng.wait_ge(*jobs.is_filled(f"ok{a}"))
                o = jobs.bank(f"ok{a}")
                A(o_k[0:64, 2 * a, :], o[0:64, :], ACT.Copy).then_inc(*act.steps())
                A(o_k[0:64, 2 * a + 1, :], o[64:128, :], ACT.Copy).then_inc(*act.frees(f"ok{a}"))
            for c in range(4):
                eng.wait_ge(*jobs.is_filled(f"ov{c}"))
                o = jobs.bank(f"ov{c}")
                A(o_v[:, c, :], o[:, :], ACT.Copy).then_inc(*act.frees(f"ov{c}"))
            for a in range(4):
                eng.wait_ge(*jobs.is_filled(f"oq{a}"))
                o = jobs.bank(f"oq{a}")
                A(flat(o_q[0:96, 2 * a:2 * a + 2, :]), o[0:96, :], ACT.Copy).then_inc(*act.frees(f"oq{a}"))
            for a in range(2):
                eng.wait_ge(*jobs.is_filled(f"ogc{a}"))
                o = jobs.bank(f"ogc{a}")
                A(flat(o_gc[:, 2 * a:2 * a + 2, :]), o[:, :], ACT.Copy).then_inc(*act.frees(f"ogc{a}"))
            eng.wait_ge(flag("q_normed"), 1)
            eng.wait_ge(*jobs.is_filled("oq3"))
            attention("oa", ODD_TILES, o_p, o_pT, 96.0 ** -0.5, False)
            for c in range(TC):
                eng.wait_ge(*jobs.is_filled(f"oct{c}"))
                o = jobs.bank(f"oct{c}")
                A(o_cat[:, 0:4, P * c:P * c + P], o[:, :].rearrange("p (j n) -> p j n", n=P), ACT.Copy).then_inc(*act.frees(f"oct{c}"))
            routed(1, (0,), "r1", 2, "h6", [[f"oo{a}"] for a in range(4)])
            experts(1, 4)
            squares(0, xT, [[f"cb10{n}"] for n in range(4)])
            stds("out", 0)
            for c in range(TC):
                eng.wait_ge(*jobs.is_filled(f"out{c}0"))
                o = jobs.bank(f"out{c}0")
                A(stage[0][:, c, 0:512], o[:, :], ACT.Copy).then_inc(*act.frees(f"out{c}0"))

        @block.vector
        def _(eng):
            dve = Lane(jobs, flag("dve_done"), flag)
            V = nc.vector
            TT, TS, STT = V.tensor_tensor, V.tensor_scalar, V.scalar_tensor_tensor
            stds_seen = [0]

            def mod_evac(l, b):
                eng.wait_ge(*jobs.is_filled(f"modT_{l}{b}"))
                o = jobs.bank(f"modT_{l}{b}")
                v = V_BADA + 4 * b if l == "a" else V_BM + 48 * (MODL[l] - 1) + 4 * b
                eng.wait_ge(*dve.last)
                TT(mod[:, MODL[l], 4 * b:4 * b + 4, :], o[:, 0:8].rearrange("p (c s) -> p c s", s=2),
                             columns(vec[:, v:v + 4], 2), ALU.add).then_inc(*dve.frees(f"modT_{l}{b}"))

            def std_ready():
                stds_seen[0] += 1
                eng.wait_ge(flag("std"), stds_seen[0])

            def gains(s, L, c, which, gain):
                eng.wait_ge(*dve.last)
                STT(gainA[:, s, :], mod[:, L, KD * which:KD * which + KD, c], 1.0, vec[:, gain:gain + KD], ALU.add, ALU.mult).then_inc(*dve.steps())

            def normalise(tag, s, src, dst):
                std_ready()
                eng.wait_ge(*jobs.is_filled(f"{tag}_ss{s}"))
                o = jobs.bank(f"{tag}_ss{s}")
                eng.wait_ge(*dve.last)
                V.reciprocal(o[:, 0:N], o[:, 0:N]).then_inc(*dve.steps())
                eng.wait_ge(*dve.last)
                TT(dst, src[:], over(o[:, 0:N], KD), ALU.mult).then_inc(*dve.frees(f"{tag}_ss{s}"))

            def normalise_gain(tag, gain, name):
                std_ready()
                eng.wait_ge(*jobs.is_filled(f"{tag}_ss0"))
                o = jobs.bank(f"{tag}_ss0")
                eng.wait_ge(*dve.last)
                V.reciprocal(o[:, 0:N], o[:, 0:N]).then_inc(*dve.steps())
                eng.wait_ge(*dve.last)
                for k in range(KD):
                    STT(xT[:, k, :], xT[:, k, :], vec[:, gain + k:gain + k + 1], o[:, 0:N],
                        ALU.mult, ALU.mult).then_inc(*dve.raises(name))
                eng.wait_ge(*dve.last)
                V.tensor_copy(small[:, 225:226], eps).then_inc(*dve.frees(f"{tag}_ss0"))

            def affine(s, L, c, which, hname):
                eng.wait_ge(*dve.last)
                for k in range(KD // 2, KD):
                    ins = TS(hT[:, s, k, :], hT[:, s, k, :], gainA[:, s, k:k + 1], shift_of(L, which, c, k),
                             ALU.mult, ALU.add)
                ins.then_inc(*dve.raises(hname))

            def residual(job, x, n0, L, which, c):
                eng.wait_ge(*jobs.is_filled(job))
                o = jobs.bank(job)
                for j in range(2):
                    ins = STT(x[:, n0 + j, :], o[:, N * j:N * j + N], mod[:, L, KD * which + n0 + j, c:c + 1],
                              x[:, n0 + j, :], ALU.mult, ALU.add)
                ins.then_inc(*dve.frees(job))

            def raise_after(name):
                eng.wait_ge(*dve.last)
                V.tensor_copy(small[:, 225:226], eps).then_inc(*dve.raises(name))

            for i in range(V_TILES):
                n = min(P, V_END - P * i)
                eng.wait_ge(*jobs.is_filled(f"vec{i}"))
                o = jobs.bank(f"vec{i}")
                V.tensor_copy(vec[:, P * i:P * i + n], o[:, 0:n]).then_inc(*dve.frees(f"vec{i}"))
            eng.wait_ge(flag("small_set"), 1)
            for a in range(4):
                eng.wait_ge(*jobs.is_filled(f"xt1{a}"))
                o = jobs.bank(f"xt1{a}")
                V.tensor_copy(cT[:, 2 * a:2 * a + 2, :], o[:, :].rearrange("p (b n) -> p b n", b=2)).then_inc(*dve.frees(f"xt1{a}"))
            normalise("n1", 1, cT, hT[:, 1])
            normalise("n1", 0, xT, hT[:, 0])
            for b in range(4):
                mod_evac("a", b)
            for s in range(2):
                gains(s, 0, s, 1, V_N1)
            raise_after("first_gains")
            affine(1, 0, 1, 0, "h1_1_v")
            affine(0, 0, 0, 0, "h1_0_v")
            eng.wait_ge(flag("log1p"), 1)
            eng.wait_ge(*dve.last)
            STT(lg, lg, 0.0, segs[:, 0:8], ALU.min, ALU.subtract).then_inc(*dve.steps())
            eng.wait_ge(flag("ret_consts_in"), 16)
            for d in range(2):
                eng.wait_ge(*dve.last)
                ins = TT(src_ret[:, d, :, :], over(lg[:, 4 * d:4 * d + 4], 2),
                         columns(phase[:, R_SF + 2 * d:R_SF + 2 * d + 2], 4), ALU.mult)
                if d == 0:
                    ins.then_inc(*dve.steps())
            ins.then_inc(*dve.raises("source_distance"))
            eng.wait_ge(flag("source_decay"), 1)
            eng.wait_ge(*dve.last)
            TS(small[:, 104:120], small[:, 104:120], HD_SCALE, None, ALU.mult).then_inc(*dve.steps())

            def fwd(a):
                return a[0:32, :]

            def bwd(a):
                return a[32:64, ::-1]

            def gate_rows(s, which):
                eng.wait_ge(*jobs.is_filled(f"gates{s}"))
                o = jobs.bank(f"gates{s}")
                for y, r in enumerate((rI, rF)):
                    src = o[64 * y:64 * y + 64, 0:N]
                    bias = gate_bias[64 * y:64 * y + 64, :]
                    eng.wait_ge(*dve.last)
                    TS(r[0:32, :], fwd(src), bias[0:32, :], None, ALU.add).then_inc(*dve.steps())
                    eng.wait_ge(*dve.last)
                    ins = TS(r[32:64, :], bwd(src), bias[32:64, :], None, ALU.add)
                    if y == 0:
                        ins.then_inc(*dve.steps())
                ins.then_inc(*dve.frees(f"gates{s}"))
                eng.wait_ge(*dve.last)
                V.tensor_copy(small[:, 225:226], eps).then_inc(*dve.raises("forget_rows"))
                eng.wait_ge(flag("log1p"), 2 + which)
                eng.wait_ge(*dve.last)
                STT(rF[0:64, :], rF[0:64, :], 0.0, rL[0:64, :], ALU.min, ALU.subtract).then_inc(*dve.steps())
                eng.wait_ge(*dve.last)
                V.tensor_tensor_scan(rB[0:64, :], zero[0:64, :], rF[0:64, :], 0.0, ALU.add, ALU.add).then_inc(*dve.steps())

            def unflip(dst, src):
                eng.wait_ge(*dve.last)
                V.tensor_copy(dst[0:32, :], fwd(src)).then_inc(*dve.steps())
                eng.wait_ge(*dve.last)
                V.tensor_copy(dst[32:64, :], bwd(src)).then_inc(*dve.steps())

            eng.wait_ge(flag("gate_bias_in"), 64)
            gate_rows(1, 0)
            eng.wait_ge(*dve.last)
            V.tensor_copy(total[0:64, :], rB[0:64, N - 1:N]).then_inc(*dve.steps())
            eng.wait_ge(*dve.last)
            TT(rG[0:64, :], rI[0:64, :], rB[0:64, :], ALU.subtract).then_inc(*dve.steps())
            eng.wait_ge(*dve.last)
            TS(rG[0:64, :], rG[0:64, :], total[0:64, :], None, ALU.add).then_inc(*dve.steps())
            eng.wait_ge(*dve.last)
            V.tensor_reduce(mc[0:64, :], rG[0:64, :], AX, ALU.max).then_inc(*dve.steps())
            eng.wait_ge(*dve.last)
            TT(mc[0:64, :], mc[0:64, :], total[0:64, :], ALU.max).then_inc(*dve.steps())
            eng.wait_ge(*dve.last)
            TS(neg_mc[0:64, :], mc[0:64, :], -1.0, None, ALU.mult).then_inc(*dve.raises("stabilised"))
            eng.wait_ge(flag("row_exp"), 1)
            unflip(rE[0:64, :], rC[0:64, :])
            raise_after("source_rows")
            gate_rows(0, 1)
            eng.wait_ge(*dve.last)
            TT(rG[0:64, :], rI[0:64, :], rB[0:64, :], ALU.subtract).then_inc(*dve.steps())
            eng.wait_ge(*dve.last)
            V.tensor_tensor_scan(rC[0:64, :], zero[0:64, :], rG[0:64, :], mc[0:64, :], ALU.add, ALU.max).then_inc(*dve.steps())
            unflip(row_g[0:64, :], rG[0:64, :])
            unflip(row_c[0:64, :], rC[0:64, :])
            eng.wait_ge(*dve.last)
            TT(rG[0:64, :], rB[0:64, :], rC[0:64, :], ALU.add).then_inc(*dve.raises("stabilised"))
            eng.wait_ge(flag("row_exp"), 2)
            unflip(row_e[0:64, :], rG[0:64, :])
            raise_after("rows_done")
            eng.wait_ge(*jobs.is_filled("src_cols"))
            o = jobs.bank("src_cols")
            TS(wcols[:], o[:, 0:128].rearrange("p (c n) -> p c n", c=TC)[:, :, 0:36], HD_SCALE, None,
                         ALU.mult).then_inc(*dve.frees("src_cols"))
            eng.wait_ge(*jobs.is_filled("gate_cols"))
            o = jobs.bank("gate_cols")
            V.tensor_copy(gcols[:], o[:, 0:256].rearrange("p (c n) -> p c n", c=4)[:, :, 0:36]).then_inc(*dve.frees("gate_cols"))
            eng.wait_ge(*jobs.is_filled("mc_rep"))
            o = jobs.bank("mc_rep")
            V.tensor_copy(mc_rep, o[:, 0:64]).then_inc(*dve.frees("mc_rep"))
            raise_after("mc_rep")

            def ctx_keys(m, c):
                job = f"c_{('rk', 'mk')[m]}{c}"
                eng.wait_ge(*jobs.is_filled(job))
                o = jobs.bank(job)
                for d in range(2):
                    w = src_ret[:, d, c, :] if m == 0 else wcols[:, c, 32 * d:32 * d + 4]
                    ins = TT(k_src[m][d][:, c, :].rearrange("p (h n) -> p h n", h=HEADS),
                             o[:, :].rearrange("p (h n) -> p h n", h=HEADS), columns(w, P), ALU.mult)
                ins.then_inc(*dve.frees(job))

            eng.wait_ge(*dve.last)
            for m in range(2):
                for c in range(TC):
                    ctx_keys(m, c)
            for d in range(2):
                eng.wait_ge(*jobs.is_filled(f"s_ret{d}"))
                o = jobs.bank(f"s_ret{d}")
                V.tensor_copy(flat(s_ret[:, d, :, :]), o[:, :]).then_inc(*dve.frees(f"s_ret{d}"))
            for d in range(2):
                for a in range(2):
                    eng.wait_ge(*jobs.is_filled(f"s_ml{d}{a}"))
                    o = jobs.bank(f"s_ml{d}{a}")
                    V.tensor_copy(flat(s_ml[:, d, 2 * a:2 * a + 2, :]), o[:, 0:258]).then_inc(*dve.frees(f"s_ml{d}{a}"))
            for i, (n, x) in enumerate((("rk", rkT), ("rq", rqT))):
                for a in range(2):
                    job = f"swap_{n}{a}"
                    eng.wait_ge(*jobs.is_filled(job))
                    o = jobs.bank(job)
                    eng.wait_ge(*dve.last)
                    TT(o[:, :].rearrange("p (j n) -> p j n", j=2), o[:, :].rearrange("p (j n) -> p j n", j=2), over(phase[:, R_SIN:R_SIN + N], 2), ALU.mult).then_inc(*dve.steps())
                    eng.wait_ge(flag("rope_cos"), 2 * i + a + 1)
                    eng.wait_ge(*dve.last)
                    TT(flat(x[:, 2 * a:2 * a + 2, :]), flat(x[:, 2 * a:2 * a + 2, :]), o[:, :], ALU.add).then_inc(*dve.frees(job))
                    raise_after("rope_ret")
            eng.wait_ge(flag("decays_whole"), 1)
            for h in range(HEADS):
                if h >= 2:
                    eng.wait_ge(*jobs.is_filled(f"ro{h - 2}"))
                eng.wait_ge(*jobs.is_filled(f"rs{h}"))
                o = jobs.bank(f"rs{h}")
                eng.wait_ge(*dve.last)
                TT(p_ret[:, h % 2, :], o[:, :], decay[:, h, :], ALU.mult).then_inc(*dve.frees(f"rs{h}"))
                if h >= 1:
                    mod_evac("a", 4 + h - 1)
                eng.wait_ge(*jobs.is_filled(f"ro{h}"))
                o = jobs.bank(f"ro{h}")
                V.tensor_copy(ret[:, :, P * h:P * h + P], o[:, 0:N].rearrange("p (c n) -> p c n", c=TC)).then_inc(*dve.frees(f"ro{h}"))

            def ml_weights(h):
                if h >= 2:
                    eng.wait_ge(*jobs.is_filled(f"mo{h - 2}1"))
                for d in range(2):
                    eng.wait_ge(*jobs.is_filled(f"cr{h}{d}"))
                    o = jobs.bank(f"cr{h}{d}")
                    g = [gcols[:, s, 32 * d + h:32 * d + h + 1] for s in range(TC)]
                    w = p_ml[:, h % 2, d, :]
                    if d == 0:
                        eng.wait_ge(*dve.last)
                        TS(w[:, 0:256], o[:, 0:256], g[0], 0.0, ALU.subtract, ALU.max).then_inc(*dve.steps())
                        ins = TS(w[:, 256:384], o[:, 128:256], g[1], 0.0, ALU.subtract, ALU.max)
                    else:
                        eng.wait_ge(*dve.last)
                        TS(w[:, 0:128], o[:, 0:128], g[0], 0.0, ALU.subtract, ALU.max).then_inc(*dve.steps())
                        ins = TS(w[:, 128:384], o[:, 0:256], g[1], 0.0, ALU.subtract, ALU.max)
                    ins.then_inc(*dve.raises("ml_w"))
                eng.wait_ge(*jobs.is_filled(f"ms{h}"))
                o = jobs.bank(f"ms{h}")
                for d in range(2):
                    eng.wait_ge(flag("ml_masked"), 2 * h + d + 1)
                    w = p_ml[:, h % 2, d, :]
                    cut = 256 if d == 0 else 128
                    eng.wait_ge(*dve.last)
                    TT(w[:, 0:cut], w[:, 0:cut], o[:, 0:cut], ALU.mult).then_inc(*dve.steps())
                    eng.wait_ge(*dve.last)
                    ins = TT(w[:, cut:384], w[:, cut:384], o[:, 128 + cut:512], ALU.mult)
                    if d == 0:
                        ins.then_inc(*dve.steps())
                ins.then_inc(*dve.frees(f"ms{h}"))

            def ml_out(h):
                for c in range(TC):
                    job = f"mo{h}{c}"
                    i = (2 * h + c) % 4
                    eng.wait_ge(*jobs.is_filled(job))
                    o = jobs.bank(job)
                    eng.wait_ge(flag("abs_den"), 2 * h + c + 1)
                    e = gcols[:, 2 + c, h:h + 33:32]
                    eng.wait_ge(*dve.last)
                    TT(dn[:, i, :], dn[:, i, :], e, ALU.max).then_inc(*dve.steps())
                    eng.wait_ge(*dve.last)
                    V.reciprocal(dn[:, i, :], dn[:, i, :]).then_inc(*dve.steps())
                    y = ml[:, c, P * h:P * h + P]
                    eng.wait_ge(*dve.last)
                    TS(y, o[:, 0:P], dn[:, i, 0:1], None, ALU.mult).then_inc(*dve.steps())
                    eng.wait_ge(*dve.last)
                    STT(y, o[:, 129:257], dn[:, i, 1:2], y, ALU.mult, ALU.add).then_inc(*dve.frees(job))

            ml_weights(0)
            mod_evac("a", 7)
            for h in range(HEADS):
                if h >= 1:
                    mod_evac("a", 8 + h - 1)
                ml_out(h)
                if h + 1 < HEADS:
                    ml_weights(h + 1)
            raise_after("ml_done")
            mod_evac("a", 11)
            for m, y in enumerate((ret, ml)):
                eng.wait_ge(flag("head_std"), m + 1)
                eng.wait_ge(*dve.last)
                V.reciprocal(segs[:, 8 * m:8 * m + 8], segs[:, 8 * m:8 * m + 8]).then_inc(*dve.steps())
                y4 = y.rearrange("p c (h n) -> p (c h) n", h=HEADS)
                eng.wait_ge(*dve.last)
                ins = TT(y4, y4, columns(segs[:, 8 * m:8 * m + 8], P), ALU.mult)
                if m == 0:
                    ins.then_inc(*dve.steps())
                    eng.wait_ge(*dve.last)
                    ins = TT(y, y, rg, ALU.mult)
                ins.then_inc(*dve.raises("y_normed"))
            for a in range(2):
                eng.wait_ge(*jobs.is_filled(f"yT1{a}"))
                o = jobs.bank(f"yT1{a}")
                V.tensor_copy(flat(yT[:, 4 + 2 * a:6 + 2 * a, :]), o[:, :]).then_inc(*dve.frees(f"yT1{a}"))
            eng.wait_ge(*jobs.is_drained("bg31"))
            for n in range(KD):
                eng.wait_ge(*jobs.is_filled(f"up{n}"))
                o = jobs.bank(f"up{n}")
                TT(merged[:, n, :], o[:, 0:N], sig_r[:, n, :], ALU.mult).then_inc(*dve.steps())
                TT(sig_m[:, n, :], o[:, N:2 * N], sig_m[:, n, :], ALU.mult).then_inc(*dve.frees(f"up{n}"))
            for a in range(4):
                residual(f"wo{a}", xT, 2 * a, 0, 2, 0)
            gains(0, 0, 0, 4, V_N2)
            normalise("n2", 0, xT, hT[:, 0])
            affine(0, 0, 0, 3, "h2_0_v")
            for b in range(KF // 2):
                for a in range(2):
                    j = 2 * b + a
                    eng.wait_ge(*jobs.is_filled(f"fi{j}"))
                    o = jobs.bank(f"fi{j}")
                    eng.wait_ge(flag("ffn_silu"), j + 1)
                    TT(f_g[:, j, :], f_sil[:, j % 2, :], o[:, N:2 * N], ALU.mult).then_inc(*dve.frees(f"fi{j}"))
                if b >= 1:
                    mod_evac("b", b - 1)
            mod_evac("b", 10)
            for b in range(KD):
                eng.wait_ge(*jobs.is_filled(f"fo{b}"))
                o = jobs.bank(f"fo{b}")
                STT(xT[:, b, :], o[:, 0:N], mod[:, 0, 40 + b, 0:1], xT[:, b, :], ALU.mult, ALU.add).then_inc(*dve.frees(f"fo{b}"))
                if b == 0:
                    mod_evac("b", 11)
                if b == 3:
                    gains(1, 1, 1, 1, V_M1)
                    normalise("e1", 1, cT, hT[:, 1])
                    affine(1, 1, 1, 0, "h3_1_v")
            normalise_gain("nf", V_FG, "x1_ready")

            def sgu_norm(i):
                if i == 17:
                    eng.wait_ge(flag("gain_in"), 16)
                    eng.wait_ge(*jobs.is_drained("ew3"))
                    eng.wait_ge(*dve.last)
                    TS(lnst[:, :, 1], lnst[:, :, 0], -1.0 / 512, None, ALU.mult).then_inc(*dve.steps())
                if 18 <= i < 22:
                    c = i - 18
                    eng.wait_ge(*dve.last)
                    TS(e_w[:, c, :], e_w[:, c, :], lnst[:, c, 1:2], None, ALU.add).then_inc(*dve.steps())
                    eng.wait_ge(*dve.last)
                    STT(e_cat[:, 0, :], e_w[:, c, :], 1.0, e_w[:, c, :], ALU.mult, ALU.mult, accum_out=lnst[:, c, 2:3]).then_inc(*dve.steps())
                if i == 22:
                    raise_after("sgu_var")
                if i == 26:
                    eng.wait_ge(flag("sgu_std"), 1)
                    eng.wait_ge(*dve.last)
                    V.reciprocal(lnst[:, :, 3], lnst[:, :, 2]).then_inc(*dve.steps())
                if 26 <= i < 30:
                    c = i - 26
                    eng.wait_ge(*dve.last)
                    STT(e_w[:, c, :], e_w[:, c, :], lnst[:, c, 3:4], e_gain, ALU.mult, ALU.mult).then_inc(*dve.raises("sgu_v"))

            def attention(tag, tiles, scale, mask, with_sink, dst):
                T = len(tiles)
                for i in range(T + 4):
                    if i < T:
                        s, c, h = tiles[i]
                        eng.wait_ge(*jobs.is_filled(f"{tag}_s{i}"))
                        o = jobs.bank(f"{tag}_s{i}")
                        w = 512 if s == 0 else N
                        a = att[:, i % 8, :]
                        if mask and s == 0:
                            at, m = mask[c]
                            eng.wait_ge(*dve.last)
                            TT(o[:, at:at + P], o[:, at:at + P], m, ALU.add).then_inc(*dve.steps())
                        eng.wait_ge(*dve.last)
                        V.tensor_reduce(a[:, 0:1], o[:, 0:w], AX, ALU.max).then_inc(*dve.steps())
                        if with_sink:
                            eng.wait_ge(*dve.last)
                            TS(a[:, 0:1], a[:, 0:1], scale, sink[:, h:h + 1], ALU.mult, ALU.max).then_inc(*dve.steps())
                        eng.wait_ge(*dve.last)
                        TS(a[:, 1:2], a[:, 0:1], -1.0 if with_sink else -scale, None, ALU.mult).then_inc(*dve.raises(f"neg_max_{tag}"))
                    if i >= 4:
                        j = i - 4
                        s, c, h = tiles[j]
                        a = att[:, j % 8, :]
                        eng.wait_ge(*jobs.is_drained(f"{tag}_s{j}"))
                        if with_sink:
                            eng.wait_ge(*dve.last)
                            TT(a[:, 2:3], a[:, 2:3], a[:, 3:4], ALU.add).then_inc(*dve.steps())
                        eng.wait_ge(*dve.last)
                        V.reciprocal(a[:, 0:1], a[:, 2:3]).then_inc(*dve.steps())
                        eng.wait_ge(*jobs.is_filled(f"{tag}_o{j}"))
                        o = jobs.bank(f"{tag}_o{j}")
                        eng.wait_ge(*dve.last)
                        TS(dst[:, 2 * s + c, 64 * h:64 * h + 64], o[:, 0:64], a[:, 0:1], None, ALU.mult).then_inc(*dve.frees(f"{tag}_o{j}"))
                    if tag == "ea":
                        sgu_norm(i)
                    if tag == "ea" and i % 3 == 1 and i > 1:
                        mod_evac("c", i // 3 - 1)
                if tag == "ea":
                    mod_evac("c", 11)

            gains(0, 1, 0, 1, V_M1)
            normalise("e1", 0, xT, hT[:, 0])
            affine(0, 1, 0, 0, "h3_0_v")
            eng.wait_ge(*jobs.is_filled("e_v"))
            o = jobs.bank("e_v")
            V.tensor_copy(flat(e_v), o[:, :]).then_inc(*dve.frees("e_v"))
            eng.wait_ge(*jobs.is_filled("e_ws"))
            o = jobs.bank("e_ws")
            V.tensor_copy(flat(e_ws), o[:, :]).then_inc(*dve.frees("e_ws"))
            eng.wait_ge(flag("even_consts_in"), 16)
            cosA, sinA = phase[:, M_COS:M_COS + N], phase[:, M_SIN:M_SIN + N]

            def rope_sum(job, x, j, count, name, rows=slice(0, P)):
                eng.wait_ge(*jobs.is_filled(job))
                o = jobs.bank(job)[rows, 0:N * j]
                if j == 2:
                    o2 = o.rearrange("p (j n) -> p j n", j=2)
                    eng.wait_ge(*dve.last)
                    TT(o2, o2, over(sinA[rows, :], 2), ALU.mult).then_inc(*dve.steps())
                else:
                    eng.wait_ge(*dve.last)
                    TT(o, o, sinA[rows, :], ALU.mult).then_inc(*dve.steps())
                    o2 = o
                eng.wait_ge(flag(f"cos_{name}"), count)
                eng.wait_ge(*dve.last)
                TT(x, x, o2, ALU.add).then_inc(*dve.frees(job))
                raise_after(f"rope_{name}")

            rope_sum("esw0", e_k[:, 0:N], 1, 1, "even")
            for a in range(2):
                rope_sum(f"esw{a + 1}", e_q[:, 2 * a:2 * a + 2, 0:N], 2, a + 2, "even")
            attention("ea", EVEN_TILES, 64.0 ** -0.5,
                      [(P, phase[:, M_HI:M_HI + P]), (0, phase[:, M_LO:M_LO + P])], True, e_o)
            raise_after("att_out_even")
            for c in range(4):
                eng.wait_ge(*jobs.is_filled(f"em{c}"))
                o = jobs.bank(f"em{c}")
                for g in range(4):
                    u = e_u[:, c, P * g:P * g + P]
                    ins = STT(u, o[:, P * g:P * g + P], vec[:, V_EVB + g:V_EVB + g + 1], u, ALU.add, ALU.mult)
                ins.then_inc(*dve.frees(f"em{c}"))
            for c in range(4):
                eng.wait_ge(*jobs.is_filled(f"ect{c}1"))
                o = jobs.bank(f"ect{c}1")
                V.tensor_copy(e_cat[:, 4:8, P * c:P * c + P], o[:, :].rearrange("p (j n) -> p j n", n=P)).then_inc(*dve.frees(f"ect{c}1"))
            for n in range(KD):
                eng.wait_ge(*jobs.is_filled(f"eo{n}"))
                o = jobs.bank(f"eo{n}")
                for s, x in enumerate((xT, cT)):
                    ins = STT(x[:, n, :], o[:, N * s:N * s + N], mod[:, 1, 16 + n, s:s + 1], x[:, n, :],
                              ALU.mult, ALU.add)
                ins.then_inc(*dve.frees(f"eo{n}"))

            def routed(l, streams, tag, L):
                ns = len(streams)
                for s in streams:
                    gains(s, L, s, 4, V_M2 + 8 * l)
                for s in streams:
                    normalise(tag, s, (xT, cT)[s], hT[:, s])
                    affine(s, L, s, 3, f"h{2 * l + 4}_{s}_v")
                eng.wait_ge(*jobs.is_filled(f"rt{l}"))
                o = jobs.bank(f"rt{l}")
                m = 32 * ns
                grouped = lambda a: a.rearrange("p (g e) -> p g e", e=E)
                mxr = rt4[:, 0, 0:2 * ns]
                eng.wait_ge(*dve.last)
                V.tensor_reduce(mxr, grouped(o[:, 0:m]), AX, ALU.max).then_inc(*dve.steps())
                eng.wait_ge(*dve.last)
                TT(grouped(logit[:, 0:m]), grouped(o[:, 0:m]), columns(mxr, E), ALU.subtract).then_inc(*dve.frees(f"rt{l}"))
                eng.wait_ge(*dve.last)
                V.memset(affp[:], 0.0).then_inc(*dve.steps())
                raise_after("logits")
                eng.wait_ge(flag("router_exp"), l + 1)
                eng.wait_ge(*dve.last)
                V.tensor_reduce(mxr, grouped(logit[:, 0:m]), AX, ALU.add).then_inc(*dve.steps())
                eng.wait_ge(*dve.last)
                V.reciprocal(mxr, mxr).then_inc(*dve.steps())
                affs = aff.rearrange("p s c e -> p (s c) e")
                eng.wait_ge(*dve.last)
                TT(affs[:, 0:2 * ns, :], grouped(logit[:, 0:m]), columns(mxr, E), ALU.mult).then_inc(*dve.steps())
                for s in streams:
                    eng.wait_ge(*dve.last)
                    V.tensor_copy(affp[:, :, 32 * s:32 * s + E], aff[:, s, :, :]).then_inc(*dve.steps())
                raise_after("affinities")
                for s in streams:
                    for c in range(TC):
                        eng.wait_ge(*jobs.is_filled(f"th{l}{s}{c}0"))
                        o = jobs.bank(f"th{l}{s}{c}0")
                        V.tensor_copy(tokens_of[:, 2 * s + c, 0:512], o[:, :]).then_inc(*dve.frees(f"th{l}{s}{c}0"))
                eng.wait_ge(*jobs.is_filled(f"at{l}"))
                o = jobs.bank(f"at{l}")
                eng.wait_ge(*dve.last)
                V.tensor_copy(aw[0:48, :], o[0:48, 0:N]).then_inc(*dve.frees(f"at{l}"))
                for r in range(CAP // 8):
                    eng.wait_ge(*dve.last)
                    V.max(mx8[0:48, :], aw[0:48, :]).then_inc(*dve.steps())
                    eng.wait_ge(*dve.last)
                    V.match_replace(aw[0:48, :], in_to_replace=mx8[0:48, :], in_values=aw[0:48, :], imm_value=-1.0).then_inc(*dve.steps())
                eng.wait_ge(*dve.last)
                TS(mk[0:48, :], aw[0:48, :], -1.0, None, ALU.is_equal).then_inc(*dve.raises("chosen"))
                eng.wait_ge(*jobs.is_filled(f"mk{l}"))
                o = jobs.bank(f"mk{l}")
                eng.wait_ge(*dve.last)
                V.tensor_copy(flat(mt), o[:, 0:96]).then_inc(*dve.frees(f"mk{l}"))
                eng.wait_ge(*jobs.is_filled(f"ps{l}"))
                o = jobs.bank(f"ps{l}")
                eng.wait_ge(*dve.last)
                TT(flat(pm), o[:, 0:96], flat(mt), ALU.mult).then_inc(*dve.frees(f"ps{l}"))
                for s in streams:
                    for c in range(TC):
                        S = sel_of[2 * s][:, c, :].rearrange("p (e m) -> p e m", e=E)
                        eng.wait_ge(*dve.last)
                        TT(S, over(iota, E), columns(pm[:, c, 32 * s:32 * s + E], CAP), ALU.is_equal).then_inc(*dve.steps())
                    raise_after("selection")
                for s in streams:
                    for c in range(TC):
                        S = sel_of[2 * s][:, c, :].rearrange("p (e m) -> p e m", e=E)
                        G = sel_of[2 * s + 1][:, c, :].rearrange("p (e m) -> p e m", e=E)
                        eng.wait_ge(*dve.last)
                        TT(G, S, columns(aff[:, s, c, :], CAP), ALU.mult).then_inc(*dve.steps())
                    raise_after("weighted")
                for s in streams:
                    for k in range(0, KD, 2):
                        eng.wait_ge(*jobs.is_filled(f"ga{l}{s}{k}"))
                        o = jobs.bank(f"ga{l}{s}{k}")
                        V.tensor_copy(x_slots(l)[:, :, k, CAP * s:CAP * s + CAP],
                                                o[:, :].rearrange("p (e m) -> p e m", e=E)).then_inc(*dve.frees(f"ga{l}{s}{k}"))
                raise_after("small_free")
                for s in streams:
                    for g in range(0, 4, 2):
                        eng.wait_ge(*jobs.is_filled(f"GT{l}{s}{g}"))
                        o = jobs.bank(f"GT{l}{s}{g}")
                        V.tensor_copy(flat(GT[s][:, g:g + 2, :]), o[:, :]).then_inc(*dve.frees(f"GT{l}{s}{g}"))

            def experts(l, G):
                W = FF // G
                with eng.Fori(0, 4) as g4:
                    for i in range(4):
                        n = g4 * (4 * XJ) + (XJ * (E * l + i))
                        eng.wait_ge(flag("expert_silu"), g4 * 4 + (E * l + i + 1))
                        eng.wait_ge(flag("experts_pe"), n + 4)
                        TT(x_g[:, 0:W], x_sil[:, 0:W], banks[:, 1, 0:W], ALU.mult).then_inc(flag("expert_gated"), 1)
                        eng.wait_ge(flag("experts_pe"), n + 7)
                        for q in range(G // 2, G):
                            src = banks[P // G * q:P // G * q + CAP, 3, 0:W]
                            ins = V.tensor_copy(y_of[0][CAP * i:CAP * i + CAP, bass.ds(g4, 1), W * q:W * q + W],
                                                src.unsqueeze(1))
                            if G == 2:
                                src = banks[96:128, 3, 0:W]
                                ins = V.tensor_copy(y_of[1][CAP * i:CAP * i + CAP, bass.ds(g4, 1), W:2 * W],
                                                    src.unsqueeze(1))
                        ins.then_inc(flag("y_by_dve"), 1)
                dve.last = (flag("y_by_dve"), E * (l + 1))

            def combine(l, streams, L):
                for s in streams:
                    for n in range(4):
                        residual(f"cb{l}{s}{n}", (xT, cT)[s], 2 * n, L, 5, s)

            routed(0, (0, 1), "r0", 1)
            experts(0, 2)
            combine(0, (1, 0), 1)
            for s in range(2):
                gains(s, 2, s, 1, V_M1 + 8)
            for s, x in ((1, cT), (0, xT)):
                normalise("o1", s, x, hT[:, s])
                affine(s, 2, s, 0, f"h5_{s}_v")
            std_ready()
            eng.wait_ge(*jobs.is_filled("ss_kv"))
            o = jobs.bank("ss_kv")
            eng.wait_ge(*dve.last)
            V.reciprocal(o[:, :], o[:, :]).then_inc(*dve.steps())
            for j in range(2):
                eng.wait_ge(*dve.last)
                ins = STT(o_ckv[:, j, :], o_ckv[:, j, :], vec[:, V_KV + j:V_KV + j + 1], o[:, :], ALU.mult, ALU.mult)
                if j == 0:
                    ins.then_inc(*dve.steps())
            ins.then_inc(*dve.frees("ss_kv"))
            raise_after("kv_normed")
            eng.wait_ge(flag("odd_consts_in"), 16)
            std_ready()
            eng.wait_ge(*jobs.is_filled("ss_q"))
            o = jobs.bank("ss_q")
            eng.wait_ge(*dve.last)
            V.reciprocal(o[:, 0:N], o[:, 0:N]).then_inc(*dve.steps())
            for j in range(3):
                eng.wait_ge(*dve.last)
                ins = STT(o_cq[:, j, :], o_cq[:, j, :], vec[:, V_QN + j:V_QN + j + 1], o[:, 0:N], ALU.mult, ALU.mult)
                if j < 2:
                    ins.then_inc(*dve.steps())
            ins.then_inc(*dve.frees("ss_q"))
            raise_after("q_normed")
            eng.wait_ge(*jobs.is_filled("osk"))
            o = jobs.bank("osk")
            eng.wait_ge(*dve.last)
            TT(o[64:96, 0:N], o[64:96, 0:N], sinA[64:96, :], ALU.mult).then_inc(*dve.steps())
            eng.wait_ge(flag("cos_kr"), 1)
            eng.wait_ge(*dve.last)
            TT(o_kr[64:96, 0:N], o_kr[64:96, 0:N], o[64:96, 0:N], ALU.add).then_inc(*dve.frees("osk"))
            raise_after("kr_roped")
            eng.wait_ge(*dve.last)
            V.tensor_copy(o_k[64:96, 0:4, :], over(o_kr[64:96, :], 4)).then_inc(*dve.steps())
            raise_after("kr_copied")
            for a in range(4):
                rope_sum(f"osq{a}", o_q[0:96, 2 * a:2 * a + 2, :], 2, a + 1, "odd", slice(0, 96))
            attention("oa", ODD_TILES, 96.0 ** -0.5, None, False, o_o)
            raise_after("att_out_odd")
            for a in range(4):
                residual(f"oo{a}", xT, 2 * a, 2, 2, 0)
            routed(1, (0,), "r1", 2)
            experts(1, 4)
            combine(1, (0,), 2)
            normalise_gain("out", V_FG2, "out_normed")
            for c in range(TC):
                eng.wait_ge(*jobs.is_filled(f"out{c}1"))
                o = jobs.bank(f"out{c}1")
                V.tensor_copy(stage[0][:, c, 512:1024], o[:, :]).then_inc(*dve.frees(f"out{c}1"))

        @block.gpsimd
        def _(eng):
            pool = Lane(jobs, flag("pool_done"), flag)
            G = nc.gpsimd

            G.memset(small[:], 0.0).then_inc(*pool.steps())
            eng.wait_ge(*pool.last)
            G.memset(eps, EPS).then_inc(*pool.steps())
            eng.wait_ge(*pool.last)
            G.memset(sil_c[:], 0.0).then_inc(*pool.steps())
            eng.wait_ge(*pool.last)
            G.memset(zero[:], 0.0).then_inc(*pool.steps())
            eng.wait_ge(*pool.last)
            G.memset(mv[:], 1.0).then_inc(*pool.steps())
            eng.wait_ge(*pool.last)
            G.memset(vc_m[:], 1.0).then_inc(*pool.steps())
            eng.wait_ge(*pool.last)
            G.memset(mg_w[:], 0.0).then_inc(*pool.raises("small_set"))
            eng.wait_ge(flag("gate_weights_in"), 16)
            eng.wait_ge(*pool.last)
            for y in range(2):
                for d in range(2):
                    a = 8 * d + 4 * y
                    ins = G.tensor_copy(mg_w[:, :, y, 32 * d:32 * d + 4], mg_raw[:, :, a:a + 4])
            ins.then_inc(*pool.raises("gate_weights"))
            for i, (n, x) in enumerate((("rk", rkT), ("rq", rqT))):
                if n == "rq":
                    eng.wait_ge(flag("decays"), 1)
                    left, right = decay[:, :, 0:P], decay[:, :, 3 * P:4 * P]
                    eng.wait_ge(*pool.last)
                    G.tensor_tensor(left, left, over(tri_le, HEADS), ALU.mult).then_inc(*pool.steps())
                    eng.wait_ge(*pool.last)
                    G.tensor_tensor(right, right, over(tri_ge, HEADS), ALU.mult).then_inc(*pool.steps())
                    eng.wait_ge(*pool.last)
                    G.tensor_tensor(left, left, right, ALU.add).then_inc(*pool.steps())
                    eng.wait_ge(*pool.last)
                    G.tensor_copy(right, left).then_inc(*pool.raises("decays_whole"))
                for a in range(2):
                    eng.wait_ge(*jobs.is_filled(f"swap_{n}{a}"))
                    eng.wait_ge(*pool.last)
                    G.tensor_tensor(x[:, 2 * a:2 * a + 2, :], x[:, 2 * a:2 * a + 2, :],
                                              over(phase[:, R_COS:R_COS + N], 2), ALU.mult).then_inc(*pool.raises("rope_cos"))
            eng.wait_ge(flag("rope_ret"), 4)
            for h in range(HEADS):
                for d in range(2):
                    eng.wait_ge(flag("ret_decay"), 2 * h + d + 1)
                    G.tensor_tensor(q_ret[:, h % 2, d, :], q_ret[:, h % 2, d, :], rqT[:, h, :], ALU.mult).then_inc(*pool.raises("ret_q"))
            for h in range(HEADS):
                for d in range(2):
                    eng.wait_ge(flag("ml_weighted"), 2 * h + d + 1)
                    w = p_ml[:, h % 2, d, :].rearrange("p (b n) -> p b n", n=P)[:, 0:3:2, :]
                    G.tensor_tensor(w, w, over((tri_le, tri_ge)[d], 2), ALU.mult).then_inc(*pool.raises("ml_masked"))
                    q = q_ml[:, h % 2, d, :]
                    G.tensor_tensor(q, q, mqT[:, h, :], ALU.mult).then_inc(*pool.raises("ml_q"))
            eng.wait_ge(flag("ml_done"), 1)
            eng.wait_ge(*jobs.is_drained("x_mo1"))
            G.tensor_tensor(ml, ml, mo, ALU.mult).then_inc(*pool.raises("ml_gated"))
            for n in range(KD):
                eng.wait_ge(*jobs.is_drained(f"up{n}"))
                G.tensor_tensor(merged[:, n, :], merged[:, n, :], sig_m[:, n, :], ALU.add).then_inc(*pool.raises("merged"))
            eng.wait_ge(flag("even_consts_in"), 16)
            cosA = phase[:, M_COS:M_COS + N]
            eng.wait_ge(*jobs.is_filled("esw0"))
            G.tensor_tensor(e_k[:, 0:N], e_k[:, 0:N], cosA, ALU.mult).then_inc(*pool.raises("cos_even"))
            for a in range(2):
                eng.wait_ge(*jobs.is_filled(f"esw{a + 1}"))
                x = e_q[:, 2 * a:2 * a + 2, 0:N]
                G.tensor_tensor(x, x, over(cosA, 2), ALU.mult).then_inc(*pool.raises("cos_even"))

            def chosen_tokens(l):
                eng.wait_ge(flag("small_free"), l + 1)
                for s in ((0, 1), (0,))[l]:
                    eng.wait_ge(*jobs.is_drained(f"ga{l}{s}7"))
                xs = x_slots(l)
                M = CAP * (2 - l)
                cur = [x_cur[:, i, 0:KD * M].rearrange("p (a k m) -> p a k m", a=1, m=M) for i in range(2)]
                G.tensor_copy(cur[0], xs[:, 0:1]).then_inc(flag("expert_tokens"), 1)
                with eng.Fori(0, 7) as r:
                    for i in range(2):
                        eng.wait_ge(flag("experts_pe"), r * (2 * XJ) + (XJ * (E * l + i) + 1))
                        G.tensor_copy(cur[1 - i], xs[:, bass.ds(r * 2 + (i + 1), 1)]).then_inc(flag("expert_tokens"), 1)
                eng.wait_ge(flag("experts_pe"), XJ * (E * l + 14) + 1)
                G.tensor_copy(cur[1], xs[:, 15:16]).then_inc(flag("expert_tokens"), 1)
                pool.last = (flag("expert_tokens"), E * (l + 1))

            chosen_tokens(0)
            eng.wait_ge(flag("odd_consts_in"), 16)
            eng.wait_ge(*jobs.is_filled("osk"))
            G.tensor_tensor(o_kr[64:96, 0:N], o_kr[64:96, 0:N], cosA[64:96, :], ALU.mult).then_inc(*pool.raises("cos_kr"))
            eng.wait_ge(flag("kr_roped"), 1)
            eng.wait_ge(*pool.last)
            G.tensor_copy(o_k[64:96, 4:8, :], over(o_kr[64:96, :], 4)).then_inc(*pool.raises("kr_copied_by_pool"))
            for a in range(4):
                eng.wait_ge(*jobs.is_filled(f"osq{a}"))
                eng.wait_ge(*pool.last)
                x = o_q[0:96, 2 * a:2 * a + 2, :]
                G.tensor_tensor(x, x, over(cosA[0:96, :], 2), ALU.mult).then_inc(*pool.raises("cos_odd"))
            eng.wait_ge(*jobs.is_drained("ohh1"))
            eng.wait_ge(*pool.last)
            G.tensor_tensor(o_gc, o_gc, o_hh, ALU.mult).then_inc(*pool.steps())
            w = [[vec[:, V_CONV + 4 * j + c:V_CONV + 4 * j + c + 1] for c in range(4)] for j in range(3)]
            out3 = o_cat[:, 4:8, :]
            for c in range(4):
                eng.wait_ge(*pool.last)
                G.tensor_scalar(o_hh[:, c, :], o_gc[:, c, :], w[0][c], None, ALU.mult).then_inc(*pool.steps())
                eng.wait_ge(*pool.last)
                G.tensor_scalar(out3[:, c, :], o_gc[:, c, :], w[1][c], None, ALU.mult).then_inc(*pool.steps())
                eng.wait_ge(*pool.last)
                G.tensor_tensor(out3[:, c, 1:N], out3[:, c, 1:N], o_hh[:, c, 0:N - 1], ALU.add).then_inc(*pool.steps())
                eng.wait_ge(*pool.last)
                G.tensor_scalar(o_hh[:, c, :], o_gc[:, c, :], w[2][c], None, ALU.mult).then_inc(*pool.steps())
                eng.wait_ge(*pool.last)
                G.tensor_tensor(out3[:, c, 0:N - 1], out3[:, c, 0:N - 1], o_hh[:, c, 1:N], ALU.add).then_inc(*pool.steps())
            eng.wait_ge(*jobs.is_drained("ogb1"))
            eng.wait_ge(*pool.last)
            G.tensor_tensor(out3, out3, o_gb, ALU.mult).then_inc(*pool.raises("conv"))
            chosen_tokens(1)


_INS = ["x", "c", "ctx", "c_ctx", "w_ada", "b_ada", "norm1_gain", "norm2_gain", "w_in", "mlstm_gate_bias",
        "ret_decay_logit", "w_ret_up", "w_ml_up", "w_out", "w_ffn_in", "w_ffn_out", "final_gain", "c_2", "ctx_2",
        "c_ctx_2", "mod_w_2", "mod_b_2", "norm1_g_2", "norm2_g_2", "ev_w_in_2", "ev_sink_2", "ev_sgu_norm_g_2",
        "ev_sgu_w_2", "ev_sgu_b_2", "ev_w_out_2", "od_w_in_2", "od_q_norm_g_2", "od_w_uq_2", "od_kv_norm_g_2",
        "od_w_ukv_2", "od_conv_w_2", "od_w_out_2", "router_w_2", "exp_w1_2", "exp_w3_2", "exp_w2_2", "final_g_2"]


def kernel(**inputs):
    import concourse.bacc as _bacc
    from concourse.bass_utils import run_bass_kernel_spmd as _run

    nc = _bacc.Bacc("TRN2", target_bir_lowering=False, num_devices=1)
    arrays, t = {}, {}
    named = {name: np.ascontiguousarray(inputs[name]) for name in _INS}
    named.update(shape_constants())
    for name, a in named.items():
        arrays[f"in_{name}_dram"] = a
        t[name] = nc.dram_tensor(f"in_{name}_dram", a.shape, mybir.dt.from_np(a.dtype), kind="ExternalInput").ap()
    out = nc.dram_tensor("out_0_dram", (1, N, D), F32, kind="ExternalOutput").ap()
    two_blocks(nc, t, out)
    r = _run(nc, [arrays], core_ids=[0])
    return r.results[0]["out_0_dram"]
```
